# Optimizing a Trainium2 kernel written in Bass

```python
import math
import jax, jax.numpy as jnp
from jax import lax
import numpy as np

D_MODEL = 1024
BATCH = 1
SEQ = 256
DEPTH = 2

N_MIXERS = 2
PLE_DIM = 256
FFN_HIDDEN = ((8 * D_MODEL // 3 + 255) // 256) * 256
DA_HEADS = 8
DA_HEAD_DIM = D_MODEL // (2 * DA_HEADS)
Q_BLOCK = 128
NA_HEADS = 16
NA_HEAD_DIM = D_MODEL // NA_HEADS
GRID_W = 64
NA_KR = 8
NA_KC = 16
NORM_EPS = 1e-6
SUBLN_EPS = 1e-5


def rmsnorm(x, g, eps=NORM_EPS):
    xf = x.astype(jnp.float32)
    y = xf * lax.rsqrt(jnp.mean(xf * xf, axis=-1, keepdims=True) + eps)
    return (y * g.astype(jnp.float32)).astype(x.dtype)

def alibi_slopes(n_heads):
    return jnp.array([2.0 ** (-8.0 * (h + 1) / n_heads) for h in range(n_heads)], dtype=jnp.float32)

def diff_attention(h, w_qkv, w_o, lq1, lk1, lq2, lk2, subln, layer_idx):
    B, S, _ = h.shape
    qkv = h @ w_qkv
    q, k, v = jnp.split(qkv, 3, axis=-1)
    q = q.reshape(B, S, DA_HEADS, 2, DA_HEAD_DIM).transpose(3, 0, 2, 1, 4)
    k = k.reshape(B, S, DA_HEADS, 2, DA_HEAD_DIM).transpose(3, 0, 2, 1, 4)
    v = v.reshape(B, S, DA_HEADS, 2 * DA_HEAD_DIM).transpose(0, 2, 1, 3)
    lam_init = 0.8 - 0.6 * math.exp(-0.3 * layer_idx)
    lam = (jnp.exp(jnp.sum(lq1.astype(jnp.float32) * lk1.astype(jnp.float32)))
           - jnp.exp(jnp.sum(lq2.astype(jnp.float32) * lk2.astype(jnp.float32)))
           + lam_init)
    slopes = alibi_slopes(DA_HEADS)
    scale = DA_HEAD_DIM ** -0.5
    nblk = S // Q_BLOCK
    qb = q.reshape(2, B, DA_HEADS, nblk, Q_BLOCK, DA_HEAD_DIM).transpose(3, 0, 1, 2, 4, 5)
    kpos = jnp.arange(S)

    def block(args):
        qblk, bi = args
        qpos = bi * Q_BLOCK + jnp.arange(Q_BLOCK)
        dist = jnp.abs(qpos[:, None] - kpos[None, :]).astype(jnp.float32)
        bias = -slopes[:, None, None] * dist
        s = jnp.einsum('mbhqd,mbhkd->mbhqk', qblk, k).astype(jnp.float32) * scale + bias
        a = jax.nn.softmax(s, axis=-1)
        a = a[0] - lam * a[1]
        return jnp.einsum('bhqk,bhkd->bhqd', a.astype(v.dtype), v)

    o = lax.map(block, (qb, jnp.arange(nblk)))
    o = o.transpose(1, 0, 3, 2, 4).reshape(B, S, DA_HEADS, 2 * DA_HEAD_DIM)
    o = rmsnorm(o, subln, eps=SUBLN_EPS) * (1.0 - lam_init)
    return o.reshape(B, S, D_MODEL) @ w_o

def neighborhood_attention(h, w_qkv, b_qkv, rpb, w_o):
    B, S, _ = h.shape
    rows = S // GRID_W
    kr = min(NA_KR, rows)
    W = GRID_W
    qkv = h @ w_qkv + b_qkv
    qkv = qkv.reshape(B, rows, W, 3, NA_HEADS, NA_HEAD_DIM).transpose(3, 0, 4, 1, 2, 5)
    q = qkv[0] * (NA_HEAD_DIM ** -0.5)
    k = qkv[1]
    v = qkv[2]
    cols = jnp.arange(W)
    cstart = jnp.clip(cols - NA_KC // 2, 0, W - NA_KC)
    col_mask = (cols[None, :] >= cstart[:, None]) & (cols[None, :] < cstart[:, None] + NA_KC)
    col_off = jnp.clip(cols[None, :] - cols[:, None], -(NA_KC - 1), NA_KC - 1) + (NA_KC - 1)
    rpb_cols = rpb[:, :, col_off]
    key_mask = jnp.tile(col_mask, (1, kr))

    def row_block(r):
        rs = jnp.clip(r - kr // 2, 0, rows - kr)
        kb = lax.dynamic_slice_in_dim(k, rs, kr, axis=2).reshape(B, NA_HEADS, kr * W, NA_HEAD_DIM)
        vb = lax.dynamic_slice_in_dim(v, rs, kr, axis=2).reshape(B, NA_HEADS, kr * W, NA_HEAD_DIM)
        qr = lax.dynamic_index_in_dim(q, r, axis=2, keepdims=False)
        row_off = rs + jnp.arange(kr) - r + (NA_KR - 1)
        bias = jnp.take(rpb_cols, row_off, axis=1)
        bias = bias.transpose(0, 2, 1, 3).reshape(NA_HEADS, W, kr * W).astype(jnp.float32)
        s = jnp.einsum('bhqd,bhkd->bhqk', qr, kb).astype(jnp.float32) + bias
        s = jnp.where(key_mask, s, -jnp.inf)
        a = jax.nn.softmax(s, axis=-1)
        return jnp.einsum('bhqk,bhkd->bhqd', a.astype(vb.dtype), vb)

    o = lax.map(row_block, jnp.arange(rows))
    o = o.transpose(1, 0, 3, 2, 4).reshape(B, S, D_MODEL)
    return o @ w_o

def swiglu(h, w_gate, w_up, w_down):
    return (jax.nn.silu(h @ w_gate) * (h @ w_up)) @ w_down

def first_inputs(seed: int = 0) -> dict:
    key = jax.random.key(seed)
    ks = jax.random.split(key, 24)
    n_a = (DEPTH + 1) // 2
    n_b = DEPTH // 2
    D, F = D_MODEL, FFN_HIDDEN
    f32 = jnp.float32

    def nrm(k, shape, scale):
        return jax.random.normal(k, shape, f32) * scale

    return {
        "x": nrm(ks[0], (BATCH, SEQ, D), 1.0),
        "p": nrm(ks[1], (DEPTH, BATCH, SEQ, PLE_DIM), 1.0),
        "norm_mix": 1.0 + nrm(ks[2], (DEPTH, D), 0.05),
        "norm_ffn": 1.0 + nrm(ks[3], (DEPTH, D), 0.05),
        "norm_ple": 1.0 + nrm(ks[4], (DEPTH, D), 0.05),
        "norm_final": 1.0 + nrm(ks[5], (D,), 0.05),
        "da_w_qkv": nrm(ks[6], (n_a, D, 3 * D), D ** -0.5),
        "da_w_o": nrm(ks[7], (n_a, D, D), D ** -0.5),
        "da_lambda_q1": nrm(ks[8], (n_a, DA_HEAD_DIM), 0.1),
        "da_lambda_k1": nrm(ks[9], (n_a, DA_HEAD_DIM), 0.1),
        "da_lambda_q2": nrm(ks[10], (n_a, DA_HEAD_DIM), 0.1),
        "da_lambda_k2": nrm(ks[11], (n_a, DA_HEAD_DIM), 0.1),
        "da_subln": 1.0 + nrm(ks[12], (n_a, 2 * DA_HEAD_DIM), 0.05),
        "na_w_qkv": nrm(ks[13], (n_b, D, 3 * D), D ** -0.5),
        "na_b_qkv": nrm(ks[14], (n_b, 3 * D), 0.02),
        "na_rpb": nrm(ks[15], (n_b, NA_HEADS, 2 * NA_KR - 1, 2 * NA_KC - 1), 0.5),
        "na_w_o": nrm(ks[16], (n_b, D, D), D ** -0.5),
        "ffn_w_gate": nrm(ks[17], (DEPTH, D, F), D ** -0.5),
        "ffn_w_up": nrm(ks[18], (DEPTH, D, F), D ** -0.5),
        "ffn_w_down": nrm(ks[19], (DEPTH, F, D), F ** -0.5),
        "ple_w_proj": nrm(ks[20], (DEPTH, PLE_DIM, D), PLE_DIM ** -0.5),
        "ple_w_gate": nrm(ks[21], (DEPTH, D, D), D ** -0.5),
    }

def first_block(x, p, norm_mix, norm_ffn, norm_ple, norm_final,
              da_w_qkv, da_w_o, da_lambda_q1, da_lambda_k1, da_lambda_q2, da_lambda_k2, da_subln,
              na_w_qkv, na_b_qkv, na_rpb, na_w_o,
              ffn_w_gate, ffn_w_up, ffn_w_down, ple_w_proj, ple_w_gate):
    h = x
    for i in range(DEPTH):
        hn = rmsnorm(h, norm_mix[i])
        j = i // N_MIXERS
        if i % N_MIXERS == 0:
            mix = diff_attention(hn, da_w_qkv[j], da_w_o[j], da_lambda_q1[j], da_lambda_k1[j],
                                 da_lambda_q2[j], da_lambda_k2[j], da_subln[j], i)
        else:
            mix = neighborhood_attention(hn, na_w_qkv[j], na_b_qkv[j], na_rpb[j], na_w_o[j])
        h = h + mix
        h = h + swiglu(rmsnorm(h, norm_ffn[i]), ffn_w_gate[i], ffn_w_up[i], ffn_w_down[i])
        gate = jax.nn.sigmoid(rmsnorm(h, norm_ple[i]) @ ple_w_gate[i])
        h = h + gate * (p[i] @ ple_w_proj[i])
    return rmsnorm(h, norm_final)


DEPTH_2 = 1

N_META = 16
D_MIX = D_MODEL
HEAD_DIM = 64
D_ATTN = D_MIX // 2
N_ATTN_HEADS = D_ATTN // HEAD_DIM
D_CONV = D_MIX - D_ATTN
N_CONV_GROUPS = D_CONV // HEAD_DIM
CONV_WIDTH = 3
D_FF = 4 * D_MODEL
EPS = 1e-5
NEG_INF = -1e30
D_IN_PROJ = 3 * D_ATTN + N_ATTN_HEADS + 3 * D_CONV


def rms_norm(x, g):
    xf = x.astype(jnp.float32)
    y = xf * lax.rsqrt(jnp.mean(xf * xf, axis=-1, keepdims=True) + EPS)
    return (y * g.astype(jnp.float32)).astype(x.dtype)

def head_rms_norm(y, n_groups, g):
    b, l, c = y.shape
    yf = y.astype(jnp.float32).reshape(b, l, n_groups, c // n_groups)
    yf = yf * lax.rsqrt(jnp.mean(yf * yf, axis=-1, keepdims=True) + EPS)
    return (yf.reshape(b, l, c) * g.astype(jnp.float32)).astype(y.dtype)

def forgetting_attention(q, k, v, log_f):
    L = q.shape[1]
    cum = jnp.cumsum(log_f.astype(jnp.float32), axis=1).transpose(0, 2, 1)
    scale = HEAD_DIM ** -0.5
    n_blocks = (L - N_META) // Q_BLOCK
    bounds = [(0, N_META)] + [(N_META + i * Q_BLOCK, N_META + (i + 1) * Q_BLOCK)
                              for i in range(n_blocks)]
    outs = []
    for lo, hi in bounds:
        qb, kb, vb = q[:, lo:hi], k[:, :hi], v[:, :hi]
        s = jnp.einsum('bqhd,bkhd->bhqk', qb, kb,
                       preferred_element_type=jnp.float32) * scale
        decay = cum[:, :, lo:hi, None] - cum[:, :, None, :hi]
        causal = jnp.arange(hi)[None, :] <= jnp.arange(lo, hi)[:, None]
        s = jnp.where(causal, s + decay, NEG_INF)
        p = jax.nn.softmax(s, axis=-1)
        outs.append(jnp.einsum('bhqk,bkhd->bqhd', p.astype(vb.dtype), vb))
    return jnp.concatenate(outs, axis=1)

def causal_depthwise_conv(u, w):
    L = u.shape[1]
    up = jnp.pad(u, ((0, 0), (CONV_WIDTH - 1, 0), (0, 0)))
    y = w[0] * up[:, 0:L]
    for kk in range(1, CONV_WIDTH):
        y = y + w[kk] * up[:, kk:kk + L]
    return y

def second_inputs(seed: int = 0) -> dict:
    key = jax.random.key(seed)
    ks = jax.random.split(key, 14)
    f32 = jnp.float32
    x = jax.random.normal(ks[0], (BATCH, SEQ, D_MODEL), f32)
    meta_tokens = jax.random.normal(ks[1], (N_META, D_MODEL), f32)
    norm_mix_g = 1.0 + 0.02 * jax.random.normal(ks[2], (DEPTH_2, D_MODEL), f32)
    w_in = jax.random.normal(ks[3], (DEPTH_2, D_MODEL, D_IN_PROJ), f32) * D_MODEL ** -0.5
    b_f = (jnp.linspace(1.0, 6.0, N_ATTN_HEADS, dtype=f32)[None, :]
           + 0.1 * jax.random.normal(ks[4], (DEPTH_2, N_ATTN_HEADS), f32))
    conv_w = jax.random.normal(ks[5], (DEPTH_2, CONV_WIDTH, D_CONV), f32) * CONV_WIDTH ** -0.5
    out_norm_g = 1.0 + 0.02 * jax.random.normal(ks[6], (DEPTH_2, D_MIX), f32)
    w_out = jax.random.normal(ks[7], (DEPTH_2, D_MIX, D_MODEL), f32) * D_MIX ** -0.5
    norm_mlp_g = 1.0 + 0.02 * jax.random.normal(ks[8], (DEPTH_2, D_MODEL), f32)
    w_ff1 = jax.random.normal(ks[9], (DEPTH_2, D_MODEL, D_FF), f32) * D_MODEL ** -0.5
    w_ff2 = jax.random.normal(ks[10], (DEPTH_2, D_FF, D_MODEL), f32) * D_FF ** -0.5
    final_norm_g = 1.0 + 0.02 * jax.random.normal(ks[11], (D_MODEL,), f32)
    return {"x": x, "meta_tokens": meta_tokens, "norm_mix_g": norm_mix_g, "w_in": w_in,
            "b_f": b_f, "conv_w": conv_w, "out_norm_g": out_norm_g, "w_out": w_out,
            "norm_mlp_g": norm_mlp_g, "w_ff1": w_ff1, "w_ff2": w_ff2,
            "final_norm_g": final_norm_g}

def second_block(x, meta_tokens, norm_mix_g, w_in, b_f, conv_w, out_norm_g, w_out,
              norm_mlp_g, w_ff1, w_ff2, final_norm_g):
    B = x.shape[0]
    meta = jnp.broadcast_to(meta_tokens.astype(x.dtype)[None], (B, N_META, D_MODEL))
    h = jnp.concatenate([meta, x], axis=1)
    L = h.shape[1]
    split_at = [D_ATTN, 2 * D_ATTN, 3 * D_ATTN, 3 * D_ATTN + N_ATTN_HEADS,
                3 * D_ATTN + N_ATTN_HEADS + D_CONV, 3 * D_ATTN + N_ATTN_HEADS + 2 * D_CONV]
    for layer in range(DEPTH_2):
        xn = rms_norm(h, norm_mix_g[layer])
        proj = jnp.einsum('bld,de->ble', xn, w_in[layer])
        q, k, v, f_logit, b_gate, c_gate, u = jnp.split(proj, split_at, axis=-1)
        log_f = jax.nn.log_sigmoid(f_logit.astype(jnp.float32) + b_f[layer].astype(jnp.float32))
        hs = (B, L, N_ATTN_HEADS, HEAD_DIM)
        y_attn = forgetting_attention(q.reshape(hs), k.reshape(hs), v.reshape(hs), log_f)
        y_attn = y_attn.reshape(B, L, D_ATTN)
        y_conv = b_gate * causal_depthwise_conv(c_gate * u, conv_w[layer].astype(u.dtype))
        y = jnp.concatenate([head_rms_norm(y_attn, N_ATTN_HEADS, out_norm_g[layer, :D_ATTN]),
                             head_rms_norm(y_conv, N_CONV_GROUPS, out_norm_g[layer, D_ATTN:])],
                            axis=-1)
        h = h + jnp.einsum('ble,ed->bld', y, w_out[layer])
        hn = rms_norm(h, norm_mlp_g[layer])
        a = jnp.square(jax.nn.relu(jnp.einsum('bld,df->blf', hn, w_ff1[layer])))
        h = h + jnp.einsum('blf,fd->bld', a, w_ff2[layer])
    h = rms_norm(h, final_norm_g)
    return h[:, N_META:]


def setup_inputs(seed=0):
    out = dict(first_inputs(seed))
    for name, value in second_inputs(seed + 1).items():
        if name != "x":
            out[name + "_2"] = value
    return out


def reference(
    x, p, norm_mix, norm_ffn, norm_ple, norm_final, da_w_qkv, da_w_o, da_lambda_q1,
    da_lambda_k1, da_lambda_q2, da_lambda_k2, da_subln, na_w_qkv, na_b_qkv, na_rpb, na_w_o,
    ffn_w_gate, ffn_w_up, ffn_w_down, ple_w_proj, ple_w_gate, meta_tokens_2, norm_mix_g_2,
    w_in_2, b_f_2, conv_w_2, out_norm_g_2, w_out_2, norm_mlp_g_2, w_ff1_2, w_ff2_2,
    final_norm_g_2,
):
    x = first_block(
        x, p, norm_mix, norm_ffn, norm_ple, norm_final, da_w_qkv, da_w_o, da_lambda_q1,
        da_lambda_k1, da_lambda_q2, da_lambda_k2, da_subln, na_w_qkv, na_b_qkv, na_rpb, na_w_o,
        ffn_w_gate, ffn_w_up, ffn_w_down, ple_w_proj, ple_w_gate,
    )
    return second_block(
        x, meta_tokens_2, norm_mix_g_2, w_in_2, b_f_2, conv_w_2, out_norm_g_2, w_out_2,
        norm_mlp_g_2, w_ff1_2, w_ff2_2, final_norm_g_2,
    )


_drawn_inputs = setup_inputs


def setup_inputs(seed=0):
    import zlib

    import numpy as np

    out = dict(_drawn_inputs(seed))
    spreads = {}
    factors = {'norm_ple': 4.416,
     'da_lambda_k1': 8.0,
     'da_lambda_q2': 8.0,
     'out_norm_g_2': 3.834,
     'norm_mlp_g_2': 3.586,
     'final_norm_g_2': 2.697}
    for name, (base, spread) in spreads.items():
        noise = np.random.default_rng([zlib.crc32(name.encode()), seed]).standard_normal(out[name].shape)
        drawn = base * np.exp(spread * noise) if base else spread * noise
        out[name] = __import__('jax').numpy.asarray(drawn.astype(out[name].dtype))
    for name, factor in factors.items():
        out[name] = (out[name] * factor).astype(out[name].dtype)
    return out
```

```python
import math
from contextlib import ExitStack

import concourse.bass as bass
from concourse import mybir

ALU = mybir.AluOpType
ACT = mybir.ActivationFunctionType
F32 = mybir.dt.float32
F32R = mybir.dt.float32r
AX_X = mybir.AxisListType.X

P = 128
D = 1024
S = 256
TB = S // P
META = 16
T = META + S
KD = D // P
UNIT = 2048
RAW = 4
RING = 4
LAYERS = 2
FFN = 2816
FF2 = 4096
EPS = 1e-6
EPS_HEAD = 1e-5
EPS_2 = 1e-5
HEAD_SCALE = 0.125
MASKED = -1e30
GRID = 64
KR, KC = 8, 16
NEAR = 384


class Order:

    def __init__(self, sem, keys):
        self.sem = sem
        self.place = {k: n + 1 for n, k in enumerate(keys)}
        assert len(self.place) == len(keys)

    def nth(self, *key):
        return self.place[key]


def two_blocks_kernel(nc, t, out):
    ctx = ExitStack()
    with ctx:
        def sb(name, shape, dt=F32):
            return ctx.enter_context(nc.sbuf_tensor(name, shape, dt))

        def sem(name):
            return ctx.enter_context(nc.semaphore(name))

        units = []

        def add_cols(w, n0, width=512):
            wv = w.rearrange("(k p) n -> p k n", p=P)
            for kh in range(2):
                units.append([(0, 512, wv[:, 4 * kh:4 * kh + 4, n0:n0 + width])])

        def add_gate_up(wg, wu, n0):
            g, u = (w.rearrange("(k p) n -> p k n", p=P) for w in (wg, wu))
            for kh in range(2):
                units.append([(0, 256, g[:, 4 * kh:4 * kh + 4, n0:n0 + 256]),
                              (256, 512, u[:, 4 * kh:4 * kh + 4, n0:n0 + 256])])

        def add_rows(w, k0):
            units.append([(0, 1024, w.rearrange("(k p) n -> p k n", p=P)[:, k0:k0 + 2, :])])

        first = {}
        ffn_shape = {}
        for l in range(LAYERS):
            wqkv = t["da_w_qkv"][0] if l == 0 else t["na_w_qkv"][0]
            wo = t["da_w_o"][0] if l == 0 else t["na_w_o"][0]
            for c in range(2):
                for part in range(3):
                    first["qkv", l, c, part] = len(units)
                    add_cols(wqkv, part * D + c * 512)
            first["wo", l] = len(units)
            for n in range(2):
                add_cols(wo, n * 512)
            first["pp", l] = len(units)
            add_rows(t["ple_w_proj"][l], 0)
            n_it = FFN // 256
            ffn_shape[l] = (n_it, 2, 1)
            for j in range(n_it + 1):
                if j < n_it:
                    first["up", l, j] = len(units)
                    add_gate_up(t["ffn_w_gate"][l], t["ffn_w_up"][l], j * 256)
                if j >= 1:
                    first["down", l, j - 1] = len(units)
                    add_rows(t["ffn_w_down"][l], 2 * (j - 1))
            first["gate", l] = len(units)
            for n in range(2):
                add_cols(t["ple_w_gate"][l], n * 512)
        w_in = t["w_in_2"][0]
        col_of = {"q": 0, "k": 512, "v": 1024, "f": 1536, "b": 1544, "c": 2056, "u": 2568}
        for part in "qkvbcu":
            first["in", part] = len(units)
            add_cols(w_in, col_of[part])
        first["wo", 2] = len(units)
        for n in range(2):
            add_cols(t["w_out_2"][0], n * 512)
        n_it = FF2 // 512
        ffn_shape[2] = (n_it, 4, 2)
        for j in range(n_it + 1):
            if j < n_it:
                first["up", 2, j] = len(units)
                add_cols(t["w_ff1_2"][0], j * 512)
            if j >= 1:
                first["down", 2, j - 1] = len(units)
                add_rows(t["w_ff2_2"][0], 4 * (j - 1))
                add_rows(t["w_ff2_2"][0], 4 * (j - 1) + 2)
        NU = len(units)

        raw = sb("raw", [P, RAW, UNIT])
        wh = sb("wh", [P, RING, UNIT], F32R)
        wl = sb("wl", [P, RING, UNIT], F32R)
        h = sb("h", [P, TB, D])
        hn = sb("hn", [P, TB, D])
        xh = sb("xh", [P, KD, T], F32R)
        xl = sb("xl", [P, KD, T], F32R)
        gains = sb("gains", [P, 2, D])
        q_reg = sb("q_reg", [P, 2048])
        k_reg = sb("k_reg", [P, 2176])
        v_reg = sb("v_reg", [P, 2048])
        b_reg = sb("b_reg", [P, 16 * NEAR])
        ah = sb("ah", [P, 1024], F32R)
        al = sb("al", [P, 1024], F32R)
        p_in = sb("p_in", [P, 512])
        prob = sb("prob", [P, 2, 512])
        pt = sb("pt", [P, 2, 512])
        ident = sb("ident", [P, P])
        groups = sb("groups", [P, P])
        stat = sb("stat", [P, 64])
        mean = sb("mean", [P, 32])
        tmps = sb("tmps", [P, 32])
        eps_c = sb("eps_c", [P, 2])
        hst_m = sb("hst_m", [P, 2, 16])
        hst_t = sb("hst_t", [P, 2, 16])
        hst = sb("hst", [P, 2, 16])
        row_sum = sb("row_sum", [P, 2, 16])
        row_inv = sb("row_inv", [P, 2, 16])
        row_max = sb("row_max", [P, 2, 2])
        row_neg = sb("row_neg", [P, 2, 2])
        lam = sb("lam", [P, 4])
        bias_q = sb("bias_q", [P, 16])
        bias_q8 = sb("bias_q8", [P, 8])
        wf_raw = sb("wf_raw", [P, KD, 8])
        conv_w = sb("conv_w", [P, 3, 4])
        conv_g = sb("conv_g", [P, 4])
        bf = sb("bf", [8, 1])

        bank = [ctx.enter_context(nc.psum_tensor(f"bank{i}", [P, 512], F32)) for i in range(8)]

        q_t = q_reg[:, :].rearrange("p (g s) -> p g s", g=8)
        k_t = k_reg[:, 0:2048].rearrange("p (g s) -> p g s", g=8)
        pp = k_reg[:, 0:2048].rearrange("p (b n) -> p b n", b=TB)
        v_s = v_reg[:, :].rearrange("p (b n) -> p b n", b=TB)
        near = b_reg[:, :].rearrange("p (h m) -> p h m", h=16)
        e_s = q_reg[:, 0:1024].rearrange("p (b n) -> p b n", b=TB)
        a_s = v_reg[:, 0:1024].rearrange("p (b n) -> p b n", b=TB)
        p_s = p_in[:, :].rearrange("p (b n) -> p b n", b=TB)
        lams = pt[:, 0, 0:256].rearrange("p (v d) -> p v d", v=4)
        lam_out = pt[:, 0, 256:320]
        sub_gain = sb("sub_gain", [P, 128])
        dist_i = b_reg[:, 8 * NEAR:9 * NEAR].bitcast(mybir.dt.int32)
        dist_f = b_reg[:, 9 * NEAR:10 * NEAR]
        dist_n = b_reg[:, 10 * NEAR:11 * NEAR]
        meta_gain = v_reg[0:META, 0:D]
        grid_mask = sb("grid_mask", [P, GRID])
        bias_v = hn[:, 0, :]
        q2 = q_reg[:, 0:1024].rearrange("p (g s) -> p g s", g=4)
        sq2 = q_reg[:, 1024:2048].rearrange("p (g s) -> p g s", g=4)
        k2 = k_reg[:, 0:4 * T].rearrange("p (g s) -> p g s", g=4)
        minus = k_reg[0:8, 4 * T:4 * T + 1024].rearrange("p (h m) -> p h m", h=8)
        v2 = v_reg[:, 0:1024].rearrange("p (b n) -> p b n", b=TB)
        o = 0
        causal = b_reg[:, o:o + 2 * T].rearrange("p (b s) -> p b s", b=2); o += 2 * T
        c_s = b_reg[:, o:o + 4 * T].rearrange("p (g s) -> p g s", g=4); o += 4 * T
        b_s = b_reg[:, o:o + 1024].rearrange("p (g s) -> p g s", g=4); o += 1024
        cu = b_reg[:, o:o + 4 * T].rearrange("p (g s) -> p g s", g=4); o += 4 * T
        v_meta = b_reg[0:META, o:o + 512]; o += 512
        y_s = b_reg[:, o:o + 1024].rearrange("p (g s) -> p g s", g=4); o += 1024
        f_z = b_reg[0:8, o:o + T]; o += T
        f_e = b_reg[0:8, o:o + T]; o += T
        f_c = b_reg[0:8, o:o + T]; o += T
        assert o <= 16 * NEAR
        y_m, y_t = b_reg[:, 2 * T:2 * T + 1024], b_reg[:, 6 * T + 1024:6 * T + 2048]
        f_one = v_reg[0:8, 1024:1024 + T]
        head_g = p_in[:, :]
        wf_h = ah[:, :].rearrange("p (k m) -> p k m", k=KD)
        wf_l = al[:, :].rearrange("p (k m) -> p k m", k=KD)
        meta_s = k_reg[0:META, 0:D]
        meta_n = k_reg[0:META, D:2 * D]

        def score_bank(i, m):
            return bank[(4, 2)[i % 2] + m]

        def tok(b):
            return slice(META + b * P, META + (b + 1) * P)

        NORMS = ["mix0", "ffn0", "ple0", "mix1", "ffn1", "ple1", "fin1", "mix2", "ffn2", "fin2"]
        TURNS = []
        for l in range(3):
            TURNS += [(f"mix{l}", b, c) for b in range(2) for c in range(2)]
            TURNS += [(f"att{l}", b, c) for c in range(1 if l == 2 else 2) for b in range(2)]
            TURNS += [(f"ffn{l}", b, c) for b in range(2) for c in range(2)]
            if l < 2:
                TURNS += [(f"ple{l}", b, c) for b in range(2) for c in range(2)]
        TURNS = [("meta", 0, 0)] + TURNS
        by_norm = [("meta", 0)] + [(n, b) for n in NORMS for b in range(2)]
        ATT = [(l, i) for l in range(3) for i in range(16)]
        ITS = [(l, j, b) for l in range(3) for j in range(ffn_shape[l][0]) for b in range(2)]

        s_raw = [sem(f"raw_landed{i}") for i in range(RAW)]
        s_hi = sem("unit_hi")
        s_lo = sem("unit_lo")
        s_used = sem("unit_used")
        sumsq = Order(sem("sumsq"), by_norm)
        normed = Order(sem("normed"), by_norm)
        turned = Order(sem("turned"), TURNS)
        turned_hi = Order(sem("turned_hi"), TURNS)
        turned_lo = Order(sem("turned_lo"), TURNS)
        q_ready = Order(sem("q_ready"), [(l, c) for l in range(2) for c in range(2)] + [(2, 0)])
        k_ready = Order(sem("k_ready"), [(l, c) for l in range(2) for c in range(2)] + [(2, 0)])
        v_ready = Order(sem("v_ready"), [(l, c) for l in range(2) for c in range(2)] + [(2, 0)])
        scored = Order(sem("scored"), ATT)
        shifted = Order(sem("shifted"), ATT)
        exped = Order(sem("exped"), ATT)
        mixed = Order(sem("mixed"), [(0, i) for i in range(16)])
        p_turned = Order(sem("p_turned"), ATT)
        p_copied = Order(sem("p_copied"), ATT)
        valued = Order(sem("valued"), ATT)
        HEADS = [(l, c, b) for l in range(2) for c in range(2) for b in range(2)] + [(2, 0, b) for b in range(2)]
        head_sq = Order(sem("head_sq"), [k for k in HEADS if k[0] != 1])
        head_ss = Order(sem("head_ss"), [k for k in HEADS if k[0] != 1])
        head_root = Order(sem("head_root"), [k for k in HEADS if k[0] != 1])
        head_o = Order(sem("head_o"), [(2, 0, b) for b in range(2)])
        heads = Order(sem("heads"), HEADS)
        emb_turned = Order(sem("emb_turned"), [(l,) for l in range(2)])
        emb_hi = Order(sem("emb_hi"), [(l,) for l in range(2)])
        emb_lo = Order(sem("emb_lo"), [(l,) for l in range(2)])
        pp_done = Order(sem("pp_done"), [(l,) for l in range(2)])
        pp_ready = Order(sem("pp_ready"), [(l, b) for l in range(2) for b in range(2)])
        summed = Order(sem("summed"), [(f"{k}{l}", n) for l in range(3) for k in (("wo", "dn", "gt") if l < 2 else ("wo", "dn"))
                                       for n in ((0, 1) if k != "dn" else (0,))])
        gate_e = Order(sem("gate_e"), [(l, n, b) for l in range(2) for n in range(2) for b in range(2)])
        RES = []
        for l in range(3):
            RES += [(f"wo{l}", n, b) for n in range(2) for b in range(2)]
            RES += [(f"dn{l}", n, b) for b in range(2) for n in range(2)]
            if l < 2:
                RES += [(f"gt{l}", n, b) for n in range(2) for b in range(2)]
        added = Order(sem("added"), RES)
        up_done = Order(sem("up_done"), [(l, j) for l in range(3) for j in range(ffn_shape[l][0])])
        act_e = Order(sem("act_e"), ITS)
        act_a = Order(sem("act_a"), ITS)
        a_turned = Order(sem("a_turned"), ITS)
        a_hi = Order(sem("a_hi"), ITS)
        a_lo = Order(sem("a_lo"), ITS)
        s_dve = sem("dve_own")
        s_pe = sem("pe_own")
        s_act = sem("act_own")
        s_pool = sem("pool_own")
        s_x = sem("x_landed")
        s_gain = [sem(f"gain_landed{i}") for i in range(2)]
        s_meta = sem("meta_landed")
        s_small = sem("small_landed")
        s_lamv = sem("lambda_landed")
        s_emb = sem("emb_landed")
        s_bv = sem("bias_v_landed")
        s_rpb = sem("rpb_landed")
        s_late = sem("late_landed")
        s_ident = sem("ident_ready")
        s_dist = sem("dist_ready")
        s_alibi = sem("alibi_ready")
        s_near = sem("near_ready")
        s_lamr = sem("lambda_ready")
        s_consts2 = sem("consts2_ready")
        s_wf = sem("wf_ready")
        s_fz = sem("f_z_ready")
        s_fabs = sem("f_abs_ready")
        s_fe = sem("f_exp_ready")
        s_f1 = sem("f_plus_ready")
        s_fl = sem("f_log_ready")
        s_cum = sem("cum_ready")
        s_bc = sem("bc_copied")
        s_cu = sem("cu_ready")
        s_ysq = sem("y_sq_ready")
        s_ysum = sem("y_sum_ready")
        s_yst = sem("y_std_ready")
        s_y = sem("y_ready")
        s_yh = sem("y_hi_ready")
        s_yl = sem("y_lo_ready")
        s_store = sem("stored")

        def used(eng, u):
            eng.wait_ge(s_used, u + 1)

        block = ctx.enter_context(nc.Block())

        @block.sync
        def _(sp):
            sp.dma_start(h[:, :, :], t["x"][0].rearrange("(b p) n -> p b n", p=P)).then_inc(s_x, 16)
            for i in range(NU):
                if i >= RAW:
                    sp.wait_ge(s_lo, i - RAW + 1)
                dst = raw[:, i % RAW, :]
                dst = dst.rearrange("p (k n) -> p k n", n=1024 if units[i][0][1] == 1024 else 512)
                for c0, c1, src in units[i]:
                    sp.dma_start(dst[:, :, c0:c1], src).then_inc(s_raw[i % RAW], 16)
            for b in range(TB):
                sp.wait_ge(normed.sem, normed.nth("fin2", b))
                sp.dma_start(out[0].rearrange("(b p) n -> p b n", p=P)[:, b, :], hn[:, b, :]).then_inc(s_store, 16)
            sp.wait_ge(s_store, 16 * TB)

        landed = []
        count = [0] * RAW
        for i in range(NU):
            count[i % RAW] += 16 * len(units[i])
            landed.append(count[i % RAW])

        @block.gpsimd
        def _(pool):
            own = [0]

            def link(ins):
                own[0] += 1
                ins.then_inc(s_pool, 1)
                pool.wait_ge(s_pool, own[0])

            gain_of = [t["norm_mix"][0], t["norm_ffn"][0], t["norm_ple"][0], t["norm_mix"][1], t["norm_ffn"][1],
                       t["norm_ple"][1], t["norm_final"], t["norm_mix_g_2"][0], t["norm_mlp_g_2"][0],
                       t["final_norm_g_2"]]

            def load_gain(n):
                if n >= 2:
                    pool.wait_ge(normed.sem, normed.nth(NORMS[n - 2], 1))
                pool.dma_start(gains[:, n % 2, :], gain_of[n].partition_broadcast(P)).then_inc(s_gain[n % 2], 16)

            pool.dma_start(gains[:, 0, :], gain_of[0].partition_broadcast(P)).then_inc(s_gain[0], 16)
            link(nc.gpsimd.memset(eps_c[:, 0:1], EPS))
            link(nc.gpsimd.memset(eps_c[:, 1:2], EPS_2))
            link(nc.gpsimd.memset(ident[:, :], 0.0))
            nc.gpsimd.affine_select(out=ident[:, :], in_=ident[:, :], compare_op=ALU.not_equal, fill=1.0, base=0,
                                    pattern=[[-1, P]], channel_multiplier=1).then_inc(s_ident, 1)
            pool.dma_start(meta_s, t["meta_tokens_2"]).then_inc(s_meta, 16)
            pool.dma_start(meta_gain, t["norm_mix_g_2"][0].partition_broadcast(META)).then_inc(s_meta, 16)
            load_gain(1)
            nc.gpsimd.iota(dist_i, pattern=[[-1, NEAR]], base=P, channel_multiplier=1).then_inc(s_dist, 1)
            for v, name in enumerate(("da_lambda_q1", "da_lambda_k1", "da_lambda_q2", "da_lambda_k2")):
                pool.dma_start(lams[:, v, :], t[name][0].partition_broadcast(P)).then_inc(s_lamv, 16)
            pool.dma_start(sub_gain[:, :], t["da_subln"][0].partition_broadcast(P)).then_inc(s_small, 16)
            pool.dma_start(p_s, t["p"][0, 0].rearrange("(b p) n -> p b n", p=P)).then_inc(s_emb, 16)
            with nc.allow_non_contiguous_dma("biases and convolution weights, a few KB"):
                pool.dma_start(bias_q[:, :], t["na_b_qkv"][0, 0:2 * D].rearrange("(g p) -> p g", p=P)).then_inc(s_small, 16)
                pool.dma_start(wf_raw[:, :, :], w_in.rearrange("(k p) n -> p k n", p=P)[:, :, col_of["f"]:col_of["f"] + 8]).then_inc(s_small, 16)
                for w in range(3):
                    pool.dma_start(conv_w[:, w, :], t["conv_w_2"][0, w].rearrange("(g p) -> p g", p=P)).then_inc(s_small, 16)
                pool.dma_start(conv_g[:, :], t["out_norm_g_2"][0, 512:1024].rearrange("(g p) -> p g", p=P)).then_inc(s_small, 16)
                pool.dma_start(bf[:, :], t["b_f_2"].rearrange("a h -> h a")).then_inc(s_small, 16)
            link(nc.gpsimd.memset(grid_mask[:, :], 0.0))
            for r in range(2):
                half = grid_mask[GRID * r:GRID * r + GRID, :]
                low, high = half[:, 0:GRID - KC], half[:, KC:GRID]
                link(nc.gpsimd.affine_select(out=low, in_=low, compare_op=ALU.is_ge, fill=MASKED, base=KC // 2,
                                             pattern=[[1, GRID - KC]], channel_multiplier=-1))
                link(nc.gpsimd.affine_select(out=high, in_=high, compare_op=ALU.is_ge, fill=MASKED,
                                             base=KC // 2 - 1 - KC, pattern=[[-1, GRID - KC]], channel_multiplier=1))
            link(nc.gpsimd.memset(groups[:, :], 0.0))
            for r in range(2):
                nc.gpsimd.memset(groups[64 * r:64 * r + 64, 64 * r:64 * r + 64], 1.0).then_inc(s_ident, 1)
                pool.wait_ge(s_ident, 2 + r)

            load_gain(2)
            pool.wait_ge(shifted.sem, shifted.nth(0, 15))
            rpb = t["na_rpb"]
            for r in range(2):
                for c in range(GRID):
                    src = bass.AP(tensor=rpb.tensor, offset=(5 - r) * 31 + KC - 1 - c,
                                  ap=[[15 * 31, 16], [31, 6], [1, GRID]])
                    row = GRID * r + c
                    pool.dma_start(near[row:row + 1, :, :].rearrange("p h (j c) -> p h j c", c=GRID),
                                   src.unsqueeze(0)).then_inc(s_rpb, 16)
            pool.wait_ge(s_rpb, 16 * P)
            for hd in range(0, 16, 4):
                part = b_reg[:, hd * NEAR:(hd + 4) * NEAR].rearrange("p (j c) -> p j c", c=GRID)
                nc.gpsimd.tensor_tensor(part, part, grid_mask[:, :].unsqueeze(1).to_broadcast([P, 24, GRID]),
                                        ALU.add).then_inc(s_near, 1)
            pool.wait_ge(s_near, 4)
            load_gain(3)
            pool.wait_ge(emb_turned.sem, emb_turned.nth(0))
            pool.dma_start(p_s, t["p"][1, 0].rearrange("(b p) n -> p b n", p=P)).then_inc(s_emb, 16)
            load_gain(4)
            pool.wait_ge(turned.sem, turned.nth("mix1", 1, 1))
            pool.dma_start(bias_v, t["na_b_qkv"][0, 2 * D:3 * D].partition_broadcast(P)).then_inc(s_bv, 16)
            load_gain(5)
            load_gain(6)
            pool.wait_ge(added.sem, added.nth("gt1", 1, 1))
            pool.dma_start(head_g, t["out_norm_g_2"][0, 0:512].partition_broadcast(P)).then_inc(s_late, 16)
            link(nc.gpsimd.memset(b_reg[:, 0:2 * T], 0.0))
            for b in range(2):
                link(nc.gpsimd.affine_select(out=causal[:, b, :], in_=causal[:, b, :], compare_op=ALU.is_ge,
                                             fill=MASKED, base=P * b + META, pattern=[[-1, T]],
                                             channel_multiplier=1))
            link(nc.gpsimd.memset(minus, 0.0))
            nc.gpsimd.affine_select(out=minus, in_=minus, compare_op=ALU.not_equal, fill=-1.0, base=0,
                                    pattern=[[-1, 8], [0, P]], channel_multiplier=1).then_inc(s_consts2, 1)
            pool.wait_ge(s_consts2, 1)
            nc.gpsimd.memset(f_one, 1.0).then_inc(s_consts2, 1)
            load_gain(7)
            load_gain(8)
            load_gain(9)

        @block.scalar
        def _(act):
            own = [0]
            split = [0]

            def link(ins):
                own[0] += 1
                ins.then_inc(s_act, 1)
                act.wait_ge(s_act, own[0])

            def split_to(n):
                while split[0] < min(n, NU):
                    i = split[0]
                    act.wait_ge(s_raw[i % RAW], landed[i])
                    if i >= RING:
                        used(act, i - RING)
                    nc.scalar.activation(wh[:, i % RING, :], raw[:, i % RAW, :], ACT.Copy).then_inc(s_hi, 1)
                    split[0] += 1

            def root(dst, total, n, eps, signal):
                link(nc.scalar.activation(dst, total, ACT.Ln, scale=1.0 / n, bias=eps))
                nc.scalar.activation(dst, dst, ACT.Exp, scale=-0.5).then_inc(signal, 1)

            def square(name, b, after):
                act.wait_ge(*after)
                i = 2 * NORMS.index(name) + b
                link(nc.scalar.activation(hn[:, b, :], h[:, b, :], ACT.Square, accum_out=stat[:, i:i + 1]))
                root(stat[:, 32 + i:33 + i], stat[:, i:i + 1], D, eps_c[:, 0:1] if name in NORMS[:7] else eps_c[:, 1:2],
                     sumsq.sem)

            def turn_hi(name, b, c):
                act.wait_ge(turned.sem, turned.nth(name, b, c))
                nc.scalar.activation(xh[:, 4 * c:4 * c + 4, tok(b)],
                                     bank[6 + c][:, :].rearrange("p (k s) -> p k s", k=4),
                                     ACT.Copy).then_inc(turned_hi.sem, 1)

            def norm_turns(name):
                for b in range(TB):
                    for c in range(2):
                        turn_hi(name, b, c)

            def after_res(stage, b):
                return added.sem, added.nth(stage, 1, b)

            act.wait_ge(s_meta, 32)
            act.wait_ge(s_ident, 1)
            link(nc.scalar.activation(meta_n, meta_s, ACT.Square, accum_out=stat[0:META, 30:31]))
            root(stat[0:META, 31:32], stat[0:META, 30:31], D, eps_c[0:META, 1:2], sumsq.sem)
            for b in range(TB):
                square("mix0", b, (s_x, 16))
            act.wait_ge(turned.sem, turned.nth("meta", 0, 0))
            nc.scalar.activation(xh[:, :, 0:META], bank[6][:, 0:P].rearrange("p (k s) -> p k s", k=KD),
                                 ACT.Copy).then_inc(turned_hi.sem, 1)
            split_to(2)
            norm_turns("mix0")
            act.wait_ge(s_lamr, 1)
            nc.scalar.activation(lam[:, 2:4], lam[:, 0:2], ACT.Exp).then_inc(s_lamr, 1)

            def attention(l):
                def exp(i):
                    g, b = i // 2, i % 2
                    act.wait_ge(shifted.sem, shifted.nth(l, i))
                    if l < 2:
                        for m in range(2):
                            ins = nc.scalar.activation(prob[:, i % 2, 256 * m:256 * m + 256], prob[:, i % 2, 256 * m:256 * m + 256],
                                                       ACT.Exp, bias=row_neg[:, i % 2, m:m + 1],
                                                       accum_out=row_sum[:, b, 2 * g + m:2 * g + m + 1])
                        ins.then_inc(exped.sem, 1)
                    else:
                        n = META + P * (b + 1)
                        nc.scalar.activation(prob[:, i % 2, 0:n], prob[:, i % 2, 0:n], ACT.Exp,
                                             bias=row_neg[:, i % 2, 0:1],
                                             accum_out=row_sum[:, b, g:g + 1]).then_inc(exped.sem, 1)

                def copy(i):
                    act.wait_ge(p_turned.sem, p_turned.nth(l, i))
                    if i >= 2:
                        act.wait_ge(valued.sem, valued.nth(l, i - 2))
                    src = bank[6 + i % 2]
                    if l == 0:
                        ins = nc.scalar.activation(pt[:, i % 2, 0:256], src[:, 0:256], ACT.Copy)
                    elif l == 1:
                        ins = nc.scalar.activation(pt[:, i % 2, :], src[:, :], ACT.Copy)
                    else:
                        n = P * (i % 2 + 1)
                        nc.scalar.activation(pt[0:META, i % 2, 256:384], src[0:META, 256:384], ACT.Copy)
                        ins = nc.scalar.activation(pt[:, i % 2, 0:n], src[:, 0:n], ACT.Copy)
                    ins.then_inc(p_copied.sem, 1)

                def head_square(c):
                    for b in range(TB):
                        if l == 0:
                            act.wait_ge(valued.sem, valued.nth(0, 8 * c + 7))
                            nc.scalar.activation(hn[:, b, 512 * c:512 * c + 512], bank[b][:, :],
                                                 ACT.Square).then_inc(head_sq.sem, 1)
                            act.wait_ge(head_ss.sem, head_ss.nth(0, c, b))
                            root(hst[:, b, 0:4], hst_m[:, b, 0:4], 128, eps_c[:, 1:2], head_root.sem)
                        elif l == 2:
                            act.wait_ge(head_o.sem, head_o.nth(2, 0, b))
                            nc.scalar.activation(hn[:, b, 512:1024], hn[:, b, 0:512],
                                                 ACT.Square).then_inc(head_sq.sem, 1)
                            act.wait_ge(head_ss.sem, head_ss.nth(2, 0, b))
                            root(hst[:, b, 0:8], hst_m[:, b, 0:8], 64, eps_c[:, 1:2], head_root.sem)

                for i in range(17):
                    if i < 16:
                        exp(i)
                    if i >= 1:
                        copy(i - 1)
                    if l < 2 and i == 10:
                        if l == 0:
                            head_square(0)
                        turn_hi(f"att{l}", 0, 0)
                        turn_hi(f"att{l}", 1, 0)
                if l == 0:
                    head_square(1)
                if l < 2:
                    turn_hi(f"att{l}", 0, 1)
                    turn_hi(f"att{l}", 1, 1)
                if l == 2:
                    head_square(0)
                    turn_hi("att2", 0, 0)
                    turn_hi("att2", 1, 0)

            def feed_forward(l):
                n_it, kt, dn = ffn_shape[l]
                for j in range(n_it):
                    u = first["up", l, j]
                    split_to(u + 2 + 3)
                    for b in range(TB):
                        if b == 0:
                            act.wait_ge(up_done.sem, up_done.nth(l, j))
                        else:
                            used(act, u + 1)
                        if l < 2:
                            ins = nc.scalar.activation(e_s[:, b, 0:256], bank[4 + b][:, 0:256], ACT.Exp, scale=-1.0)
                        else:
                            ins = nc.scalar.activation(e_s[:, b, :], bank[4 + b][:, :], ACT.Relu)
                        ins.then_inc(act_e.sem, 1)
                    split_to(u + 2 + (dn if j else 0) + 3)
                    for b in range(TB):
                        act.wait_ge(a_turned.sem, a_turned.nth(l, j, b))
                        nc.scalar.activation(ah[:, 0:256 * kt].rearrange("p (k s) -> p k s", s=S)[:, :, b * P:(b + 1) * P],
                                             bank[6 + b][:, 0:kt * P].rearrange("p (k s) -> p k s", s=P),
                                             ACT.Copy).then_inc(a_hi.sem, 1)
                split_to(first["down", l, n_it - 1] + dn + 3)

            for l in range(LAYERS):
                if l == 1:
                    norm_turns("mix1")
                for c in range(2):
                    u = first["qkv", l, c, 0]
                    split_to(u + 2 + 3)
                    used(act, u + 1)
                    for m in range(4):
                        src = bank[2 * (c % 2) + m // 2][:, 256 * (m % 2):256 * (m % 2) + 256]
                        if l == 0:
                            ins = nc.scalar.activation(q_t[:, 4 * c + m, :], src, ACT.Copy, scale=HEAD_SCALE)
                        else:
                            ins = nc.scalar.activation(q_t[:, 4 * c + m, :], src, ACT.Identity, scale=HEAD_SCALE,
                                                       bias=bias_q8[:, 4 * c + m:4 * c + m + 1])
                    ins.then_inc(q_ready.sem, 1)
                    split_to(u + 6 + 3)
                act.wait_ge(emb_turned.sem, emb_turned.nth(l))
                nc.scalar.activation(ah[:, 0:512], bank[6][:, :], ACT.Copy).then_inc(emb_hi.sem, 1)
                split_to(first["wo", l] + 4)
                attention(l)
                split_to(first["wo", l] + 4 + 3)

                def pp_out(b):
                    if b == 0:
                        act.wait_ge(pp_done.sem, pp_done.nth(l))
                    else:
                        used(act, first["pp", l])
                    nc.scalar.activation(pp[:, b, 0:512], bank[4 + 2 * b][:, :], ACT.Copy)
                    nc.scalar.activation(pp[:, b, 512:1024], bank[5 + 2 * b][:, :], ACT.Copy).then_inc(pp_ready.sem, 1)

                square(f"ffn{l}", 0, after_res(f"wo{l}", 0))
                pp_out(0)
                square(f"ffn{l}", 1, after_res(f"wo{l}", 1))
                pp_out(1)
                split_to(first["pp", l] + 1 + 3)
                norm_turns(f"ffn{l}")
                feed_forward(l)
                for b in range(TB):
                    square(f"ple{l}", b, after_res(f"dn{l}", b))
                split_to(first["gate", l] + 4)
                norm_turns(f"ple{l}")
                for n in range(2):
                    u = first["gate", l] + 2 * n
                    split_to(u + 2 + 3)
                    for b in range(TB):
                        if b == 0:
                            act.wait_ge(summed.sem, summed.nth(f"gt{l}", n))
                        else:
                            used(act, u + 1)
                        nc.scalar.activation(prob[:, b, :], bank[2 * b + n][:, :], ACT.Exp,
                                             scale=-1.0).then_inc(gate_e.sem, 1)
                        if n == 0:
                            pass
                    for b in range(TB):
                        if n == 0:
                            act.wait_ge(added.sem, added.nth(f"gt{l}", 0, b))
                nxt = "mix1" if l == 0 else "fin1"
                for b in range(TB):
                    square(nxt, b, after_res(f"gt{l}", b))
                split_to(first["gate", l] + 4 + 4)
            for b in range(TB):
                square("mix2", b, (normed.sem, normed.nth("fin1", b)))
            norm_turns("mix2")
            u = first["in", "q"]
            split_to(u + 5)
            used(act, u + 1)
            for m in range(4):
                ins = nc.scalar.activation(q2[:, m, :], bank[m // 2][:, 256 * (m % 2):256 * (m % 2) + 256],
                                           ACT.Copy, scale=HEAD_SCALE)
            ins.then_inc(q_ready.sem, 1)
            split_to(first["in", "v"] + 2 + 3)
            act.wait_ge(s_fabs, 1)
            nc.scalar.activation(f_e, f_e, ACT.Exp, scale=-1.0).then_inc(s_fe, 1)
            act.wait_ge(s_f1, 1)
            nc.scalar.activation(f_e, f_e, ACT.Ln).then_inc(s_fl, 1)
            split_to(first["in", "b"] + 2 + 3)
            used(act, first["in", "b"] + 1)
            for m in range(4):
                ins = nc.scalar.activation(b_s[:, m, :], bank[4 + m // 2][:, 256 * (m % 2):256 * (m % 2) + 256], ACT.Copy)
            ins.then_inc(s_bc, 1)
            split_to(first["in", "c"] + 2 + 3)
            used(act, first["in", "c"] + 1)
            for m in range(4):
                ins = nc.scalar.activation(c_s[:, m, :], bank[m][:, 0:T], ACT.Copy)
            ins.then_inc(s_bc, 1)
            split_to(first["in", "u"] + 2 + 3)
            attention(2)
            act.wait_ge(s_ysum, 1)
            for m in range(2):
                ins = nc.scalar.activation(q_reg[:, 1024 + 512 * m:1536 + 512 * m], bank[2 + m][:, :], ACT.Ln,
                                           scale=1.0 / 64, bias=eps_c[:, 1:2])
            link(ins)
            nc.scalar.activation(q_reg[:, 1024:2048], q_reg[:, 1024:2048], ACT.Exp, scale=-0.5).then_inc(s_yst, 1)
            act.wait_ge(s_y, 1)
            nc.scalar.activation(xh[:, 4:8, META:T], y_s, ACT.Copy).then_inc(s_yh, 1)
            split_to(first["wo", 2] + 4 + 3)
            for b in range(TB):
                square("ffn2", b, after_res("wo2", b))
            norm_turns("ffn2")
            feed_forward(2)
            for b in range(TB):
                square("fin2", b, after_res("dn2", b))

        @block.tensor
        def _(pe):
            def unit(u):
                pe.wait_ge(s_lo, u + 1)
                return wh[:, u % RING, :], wl[:, u % RING, :]

            def three(dst, lhs, rhs, start, stop, **kw):
                (lh, ll), (rh, rl) = lhs, rhs
                nc.tensor.matmul(dst, lh, rh, start=start, stop=False, skip_group_check=True, **kw)
                nc.tensor.matmul(dst, lh, rl, start=False, stop=False, skip_group_check=True, **kw)
                return nc.tensor.matmul(dst, ll, rh, start=False, stop=stop, skip_group_check=True, **kw)

            def x_of(k, cols):
                return xh[:, k, cols], xl[:, k, cols]

            def need(name, b, c):
                pe.wait_ge(turned_lo.sem, turned_lo.nth(name, b, c))

            def norm_turns(name):
                for b in range(TB):
                    pe.wait_ge(normed.sem, normed.nth(name, b))
                    for c in range(2):
                        turn(name, b, c)

            def turn(name, b, c):
                if b == 1:
                    need(name, 0, c)
                for k in range(4):
                    ins = nc.tensor.transpose(bank[6 + c][:, k * P:(k + 1) * P],
                                              hn[:, b, (4 * c + k) * P:(4 * c + k + 1) * P], ident[:, :])
                ins.then_inc(turned.sem, 1)

            def tokens_out(u0, banks, name, signal=None):
                for kh in range(2):
                    w_hi, w_lo = (w.rearrange("p (k n) -> p k n", k=4) for w in unit(u0 + kh))
                    for b in range(TB):
                        if name:
                            need(name, b, kh)
                        for k in range(4):
                            ins = three(banks[b][:, :], x_of(4 * kh + k, tok(b)), (w_hi[:, k, :], w_lo[:, k, :]),
                                        kh == 0 and k == 0, kh == 1 and k == 3)
                        if kh == 1 and b == 0 and signal:
                            ins.then_inc(signal, 1)
                    ins.then_inc(s_used, 1)

            def features_out(u0, dst, width, cols, name):
                for kh in range(2):
                    w_hi, w_lo = (w.rearrange("p (k n) -> p k n", k=4) for w in unit(u0 + kh))
                    for b in range(TB):
                        need(name, b, kh)
                    for m in range(4):
                        shared = width == 256 and m % 2 == 1
                        for k in range(4):
                            ins = three(dst(m), (w_hi[:, k, m * P:(m + 1) * P], w_lo[:, k, m * P:(m + 1) * P]),
                                        x_of(4 * kh + k, cols), kh == 0 and k == 0 and not shared,
                                        kh == 1 and k == 3)
                    ins.then_inc(s_used, 1)

            def pair(first_bank):
                return lambda m: bank[first_bank + m // 2][:, 256 * (m % 2):256 * (m % 2) + 256]

            def attention(l):
                def scores(i):
                    g, b = i // 2, i % 2
                    if i >= 2:
                        pe.wait_ge(shifted.sem, shifted.nth(l, i - 2))
                    if l < 2:
                        for m in range(2):
                            half = slice(64 * m, 64 * m + 64)
                            ins = nc.tensor.matmul(score_bank(i, m)[:, 0:256], q_t[half, g, b * P:(b + 1) * P],
                                                   k_t[half, g, :], start=True, stop=True)
                    else:
                        n = META + P * (b + 1)
                        half = slice(64 * (g % 2), 64 * (g % 2) + 64)
                        dst = bank[4 + i % 2]
                        nc.tensor.matmul(dst[:, 0:n], minus[:, g, :], f_c[:, 0:n], start=True, stop=False).then_inc(s_pe, 1)
                        pe.wait_ge(s_pe, i + 1)
                        ins = nc.tensor.matmul(dst[:, 0:n], q2[half, g // 2, b * P:(b + 1) * P], k2[half, g // 2, 0:n],
                                               start=False, stop=True)
                    ins.then_inc(scored.sem, 1)

                def turn_probs(i):
                    b = i % 2
                    if l == 0:
                        pe.wait_ge(mixed.sem, mixed.nth(0, i))
                    else:
                        pe.wait_ge(exped.sem, exped.nth(l, i))
                    if i >= 2:
                        pe.wait_ge(p_copied.sem, p_copied.nth(l, i - 2))
                    dst = bank[6 + b]
                    if l < 2:
                        for m in range(1 if l == 0 else 2):
                            for kb in range(2):
                                cols = slice(256 * m + P * kb, 256 * m + P * kb + P)
                                ins = nc.tensor.transpose(dst[:, cols], prob[:, b, cols], ident[:, :])
                    else:
                        nc.tensor.transpose(dst[0:META, 256:384], prob[:, b, 0:META], ident[:, :])
                        for kb in range(b + 1):
                            ins = nc.tensor.transpose(dst[:, P * kb:P * kb + P],
                                                      prob[:, b, META + P * kb:META + P * kb + P], ident[:, :])
                    ins.then_inc(p_turned.sem, 1)

                def values(i):
                    g, b = i // 2, i % 2
                    pe.wait_ge(p_copied.sem, p_copied.nth(l, i))
                    if l == 0:
                        dst = bank[b][:, P * (g % 4):P * (g % 4) + P]
                        for kb in range(2):
                            ins = nc.tensor.matmul(dst, pt[:, b, P * kb:P * kb + P], v_s[:, kb, P * g:P * g + P],
                                                   start=(kb == 0), stop=(kb == 1))
                    elif l == 1:
                        for m in range(2):
                            hd = 2 * g + m
                            dst = bank[b][:, 64 * (hd % 8):64 * (hd % 8) + 64]
                            for kb in range(2):
                                ins = nc.tensor.matmul(dst, pt[:, b, 256 * m + P * kb:256 * m + P * kb + P],
                                                       v_s[:, kb, 64 * hd:64 * hd + 64],
                                                       start=(kb == 0), stop=(kb == 1))
                    else:
                        dst = bank[b][:, 64 * g:64 * g + 64]
                        for kb in range(b + 1):
                            nc.tensor.matmul(dst, pt[:, b, P * kb:P * kb + P], v2[:, kb, 64 * g:64 * g + 64],
                                             start=(kb == 0), stop=False)
                        ins = nc.tensor.matmul(dst, pt[0:META, b, 256:384], v_meta[:, 64 * g:64 * g + 64],
                                               start=False, stop=True)
                    ins.then_inc(valued.sem, 1)

                for i in range(18):
                    if i < 16:
                        scores(i)
                    if 1 <= i < 17:
                        turn_probs(i - 1)
                    if l < 2 and i == 10:
                        pe.wait_ge(heads.sem, heads.nth(l, 0, 0))
                        pe.wait_ge(heads.sem, heads.nth(l, 0, 1))
                    if i >= 2:
                        values(i - 2)
                    if l < 2 and i == 10:
                        pe.wait_ge(p_copied.sem, p_copied.nth(l, 8))
                        for b in range(TB):
                            if b == 1:
                                need(f"att{l}", 0, 0)
                            head_turn(l, b, 0)
                        need(f"att{l}", 1, 0)
                c = 1 if l < 2 else 0
                for b in range(TB):
                    pe.wait_ge(heads.sem, heads.nth(l, c, b))
                    if b == 1:
                        need(f"att{l}", 0, c)
                    head_turn(l, b, c)

            def head_turn(l, b, c):
                for k in range(4):
                    ins = nc.tensor.transpose(bank[6 + c][:, k * P:(k + 1) * P],
                                              hn[:, b, (4 * c + k) * P:(4 * c + k + 1) * P], ident[:, :])
                ins.then_inc(turned.sem, 1)

            def feed_forward(l):
                n_it, kt, dn = ffn_shape[l]
                for j in range(n_it + 1):
                    if j < n_it:
                        if j >= 1:
                            for b in range(TB):
                                pe.wait_ge(act_a.sem, act_a.nth(l, j - 1, b))
                        tokens_out(first["up", l, j], (bank[4], bank[5]), f"ffn{l}", up_done.sem)
                    if j >= 1:
                        for d in range(dn):
                            w_hi, w_lo = (w.rearrange("p (k n) -> p k n", k=2) for w in unit(first["down", l, j - 1] + d))
                            for b in range(TB):
                                if d == 0:
                                    pe.wait_ge(a_lo.sem, a_lo.nth(l, j - 1, b))
                                for k in range(2):
                                    cols = slice(S * (2 * d + k) + b * P, S * (2 * d + k) + (b + 1) * P)
                                    for n in range(2):
                                        ins = three(bank[2 * b + n][:, :], (ah[:, cols], al[:, cols]),
                                                    (w_hi[:, k, 512 * n:512 * n + 512], w_lo[:, k, 512 * n:512 * n + 512]),
                                                    j == 1 and d == 0 and k == 0,
                                                    j == n_it and d == dn - 1 and k == 1)
                                if j == n_it and d == dn - 1 and b == 0:
                                    ins.then_inc(summed.sem, 1)
                            ins.then_inc(s_used, 1)
                    if j < n_it:
                        for b in range(TB):
                            pe.wait_ge(act_a.sem, act_a.nth(l, j, b))
                            if j >= 1:
                                pe.wait_ge(a_lo.sem, a_lo.nth(l, j - 1, b))
                            for k in range(kt):
                                ins = nc.tensor.transpose(bank[6 + b][:, k * P:(k + 1) * P],
                                                          a_s[:, b, k * P:(k + 1) * P], ident[:, :])
                            ins.then_inc(a_turned.sem, 1)

            pe.wait_ge(s_ident, 1)
            pe.wait_ge(normed.sem, normed.nth("meta", 0))
            for k in range(KD):
                ins = nc.tensor.transpose(bank[6][:, META * k:META * k + META], meta_n[:, k * P:(k + 1) * P],
                                          ident[0:META, 0:META])
            ins.then_inc(turned.sem, 1)
            need("meta", 0, 0)
            for l in range(LAYERS):
                norm_turns(f"mix{l}")
                for c in range(2):
                    for part in range(3):
                        i = 3 * c + part
                        if i >= 2:
                            prev = i - 2
                            o_ = (q_ready, k_ready, v_ready)[prev % 3]
                            pe.wait_ge(o_.sem, o_.nth(l, prev // 3))
                        u = first["qkv", l, c, part]
                        b0 = 2 * (i % 2)
                        if part < 2:
                            features_out(u, pair(b0), 256, slice(META, T), f"mix{l}")
                        else:
                            tokens_out(u, (bank[b0], bank[b0 + 1]), f"mix{l}")
                pe.wait_ge(s_emb, 16 * (l + 1))
                for b in range(TB):
                    for k in range(2):
                        ins = nc.tensor.transpose(bank[6][:, S * k + b * P:S * k + (b + 1) * P],
                                                  p_s[:, b, k * P:(k + 1) * P], ident[:, :])
                ins.then_inc(emb_turned.sem, 1)
                pe.wait_ge(q_ready.sem, q_ready.nth(l, 1))
                pe.wait_ge(k_ready.sem, k_ready.nth(l, 1))
                pe.wait_ge(v_ready.sem, v_ready.nth(l, 1))
                pe.wait_ge(emb_lo.sem, emb_lo.nth(l))
                attention(l)
                for n in range(2):
                    tokens_out(first["wo", l] + 2 * n, (bank[n], bank[2 + n]), f"att{l}", summed.sem)
                w_hi, w_lo = (w.rearrange("p (k n) -> p k n", k=2) for w in unit(first["pp", l]))
                for b in range(TB):
                    for n in range(2):
                        for k in range(2):
                            cols = slice(S * k + b * P, S * k + (b + 1) * P)
                            ins = three(bank[4 + 2 * b + n][:, :], (ah[:, cols], al[:, cols]),
                                        (w_hi[:, k, 512 * n:512 * n + 512], w_lo[:, k, 512 * n:512 * n + 512]),
                                        k == 0, k == 1)
                    ins.then_inc(pp_done.sem if b == 0 else s_used, 1)
                for b in range(TB):
                    pe.wait_ge(pp_ready.sem, pp_ready.nth(l, b))
                norm_turns(f"ffn{l}")
                feed_forward(l)
                norm_turns(f"ple{l}")
                for n in range(2):
                    tokens_out(first["gate", l] + 2 * n, (bank[n], bank[2 + n]), f"ple{l}", summed.sem)
            norm_turns("mix2")
            every = slice(0, T)
            features_out(first["in", "q"], pair(0), 256, slice(META, T), "mix2")
            features_out(first["in", "k"], lambda m: bank[4 + m][:, 0:T], T, every, "mix2")
            pe.wait_ge(q_ready.sem, q_ready.nth(2, 0))
            pe.wait_ge(s_wf, 2)
            for k in range(KD):
                three(bank[3][:, 0:T], (wf_h[:, k, :], wf_l[:, k, :]), x_of(k, every), k == 0, k == KD - 1)
            for kh in range(2):
                w_hi, w_lo = (w.rearrange("p (k n) -> p k n", k=4) for w in unit(first["in", "v"] + kh))
                for b, cols in enumerate((tok(0), tok(1), slice(0, P))):
                    for k in range(4):
                        ins = three(bank[b][:, :], x_of(4 * kh + k, cols), (w_hi[:, k, :], w_lo[:, k, :]),
                                    kh == 0 and k == 0, kh == 1 and k == 3)
                ins.then_inc(s_used, 1)
            pe.wait_ge(k_ready.sem, k_ready.nth(2, 0))
            features_out(first["in", "b"], pair(4), 256, slice(META, T), "mix2")
            pe.wait_ge(v_ready.sem, v_ready.nth(2, 0))
            features_out(first["in", "c"], lambda m: bank[m][:, 0:T], T, every, "mix2")
            pe.wait_ge(s_bc, 1)
            features_out(first["in", "u"], lambda m: bank[4 + m][:, 0:T], T, every, "mix2")
            pe.wait_ge(s_cu, 1)
            pe.wait_ge(s_bc, 2)
            pe.wait_ge(s_cum, 1)
            pe.wait_ge(s_consts2, 2)
            attention(2)
            pe.wait_ge(s_ysq, 1)
            pe.wait_ge(s_ident, 3)
            for m in range(4):
                ins = nc.tensor.matmul(pair(2)(m), groups[:, :], sq2[:, m, :], start=(m % 2 == 0), stop=True,
                                       skip_group_check=True)
            ins.then_inc(s_ysum, 1)
            pe.wait_ge(s_yl, 1)
            for n in range(2):
                for kh in range(2):
                    w_hi, w_lo = (w.rearrange("p (k n) -> p k n", k=4) for w in unit(first["wo", 2] + 2 * n + kh))
                    for b in range(TB):
                        if kh == 0:
                            need("att2", b, 0)
                        for k in range(4):
                            ins = three(bank[n + 2 * b][:, :], x_of(4 * kh + k, tok(b)), (w_hi[:, k, :], w_lo[:, k, :]),
                                        kh == 0 and k == 0, kh == 1 and k == 3)
                        if kh == 1 and b == 0:
                            ins.then_inc(summed.sem, 1)
                    ins.then_inc(s_used, 1)
            norm_turns("ffn2")
            feed_forward(2)

        @block.vector
        def _(dve):
            own = [0]
            split = [0]

            def link(ins):
                own[0] += 1
                ins.then_inc(s_dve, 1)
                dve.wait_ge(s_dve, own[0])

            def split_to(n):
                while split[0] < min(n, NU):
                    i = split[0]
                    dve.wait_ge(s_hi, i + 1)
                    nc.vector.tensor_tensor(wl[:, i % RING, :], raw[:, i % RAW, :],
                                            wh[:, i % RING, :].bitcast(F32), ALU.subtract).then_inc(s_lo, 1)
                    split[0] += 1

            def mean_eps(x, total, n, eps):
                link(nc.vector.tensor_scalar(x, total, 1.0 / n, eps, ALU.mult, ALU.add))

            def refine(y, x, tmp, gain=1.0):
                link(nc.vector.tensor_tensor(tmp, y, y, ALU.mult))
                link(nc.vector.tensor_tensor(tmp, tmp, x, ALU.mult))
                link(nc.vector.tensor_scalar(tmp, tmp, -0.5 * gain, 1.5 * gain, ALU.mult, ALU.add))
                link(nc.vector.tensor_tensor(y, y, tmp, ALU.mult))

            def norm(name, b, dst=None, eps=EPS):
                n = NORMS.index(name)
                dve.wait_ge(sumsq.sem, sumsq.nth(name, b))
                i = 2 * n + b
                r_ = stat[:, 32 + i:33 + i]
                mean_eps(mean[:, i:i + 1], stat[:, i:i + 1], D, eps)
                refine(r_, mean[:, i:i + 1], tmps[:, i:i + 1])
                if b == 0:
                    dve.wait_ge(s_gain[n % 2], 16 * (n // 2 + 1))
                nc.vector.scalar_tensor_tensor(out=hn[:, b, :] if dst is None else dst, in0=h[:, b, :], scalar=r_,
                                               in1=gains[:, n % 2, :], op0=ALU.mult, op1=ALU.mult).then_inc(normed.sem, 1)

            def turn_lo(name, b, c):
                dve.wait_ge(turned_hi.sem, turned_hi.nth(name, b, c))
                dst = (slice(None), slice(4 * c, 4 * c + 4), tok(b))
                nc.vector.tensor_tensor(xl[dst], bank[6 + c][:, :].rearrange("p (k s) -> p k s", k=4),
                                        xh[dst].bitcast(F32), ALU.subtract).then_inc(turned_lo.sem, 1)

            def norm_turns(name):
                for b in range(TB):
                    for c in range(2):
                        turn_lo(name, b, c)

            def add_halves(stage, u0):
                for n in range(2):
                    for b in range(TB):
                        if b == 0:
                            dve.wait_ge(summed.sem, summed.nth(stage, n))
                        else:
                            used(dve, u0 + 2 * n + 1)
                        nc.vector.tensor_tensor(h[:, b, 512 * n:512 * n + 512], h[:, b, 512 * n:512 * n + 512],
                                                bank[2 * b + n][:, :], ALU.add).then_inc(added.sem, 1)

            def attention(l):
                def shift(i):
                    g, b = i // 2, i % 2
                    dve.wait_ge(scored.sem, scored.nth(l, i))
                    if i >= 2:
                        dve.wait_ge(p_turned.sem, p_turned.nth(l, i - 2))
                    if l < 2:
                        for m in range(2):
                            hd = g if l == 0 else 2 * g + m
                            ins = nc.vector.tensor_tensor_reduce(
                                out=prob[:, i % 2, 256 * m:256 * m + 256], in0=score_bank(i, m)[:, 0:256],
                                in1=near[:, hd, P - P * b:P - P * b + 256], scale=1.0, scalar=-3.0e38,
                                op0=ALU.add, op1=ALU.max, accum_out=row_max[:, i % 2, m:m + 1])
                        link(ins)
                        nc.vector.tensor_scalar(row_neg[:, i % 2, :], row_max[:, i % 2, :], -1.0, None,
                                                ALU.mult).then_inc(shifted.sem, 1)
                    else:
                        n = META + P * (b + 1)
                        link(nc.vector.tensor_tensor_reduce(
                            out=prob[:, i % 2, 0:n], in0=bank[4 + i % 2][:, 0:n], in1=causal[:, b, 0:n], scale=1.0,
                            scalar=-3.0e38, op0=ALU.add, op1=ALU.max, accum_out=row_max[:, i % 2, 0:1]))
                        nc.vector.tensor_scalar(row_neg[:, i % 2, 0:1], row_max[:, i % 2, 0:1], -1.0, None,
                                                ALU.mult).then_inc(shifted.sem, 1)

                def mix(i):
                    g, b = i // 2, i % 2
                    dve.wait_ge(exped.sem, exped.nth(0, i))
                    r_ = row_inv[:, b, 2 * g:2 * g + 2]
                    link(nc.vector.reciprocal(r_, row_sum[:, b, 2 * g:2 * g + 2]))
                    link(nc.vector.tensor_scalar(prob[:, i % 2, 256:512], prob[:, i % 2, 256:512],
                                                 row_inv[:, b, 2 * g + 1:2 * g + 2], lam[:, 0:1], ALU.mult, ALU.mult))
                    nc.vector.scalar_tensor_tensor(out=prob[:, i % 2, 0:256], in0=prob[:, i % 2, 0:256],
                                                   scalar=row_inv[:, b, 2 * g:2 * g + 1], in1=prob[:, i % 2, 256:512],
                                                   op0=ALU.mult, op1=ALU.subtract).then_inc(mixed.sem, 1)

                def root_of(b, n, width, key, gain):
                    dve.wait_ge(head_root.sem, head_root.nth(*key))
                    mean_eps(hst_m[:, b, 0:n], hst_m[:, b, 0:n], width, EPS_2)
                    refine(hst[:, b, 0:n], hst_m[:, b, 0:n], hst_t[:, b, 0:n], gain)

                def head_out(c):
                    for b in range(TB):
                        if l == 0:
                            dve.wait_ge(head_sq.sem, head_sq.nth(0, c, b))
                            dst = hn[:, b, 512 * c:512 * c + 512].rearrange("p (h d) -> p h d", h=4)
                            src = bank[b][:, :].rearrange("p (h d) -> p h d", h=4)
                            nc.vector.tensor_reduce(hst_m[:, b, 0:4], dst, AX_X, ALU.add).then_inc(head_ss.sem, 1)
                            root_of(b, 4, 128, (0, c, b), 1.0 - LAM_INIT)
                            link(nc.vector.tensor_tensor(dst, src, hst[:, b, 0:4].unsqueeze(2).to_broadcast([P, 4, 128]),
                                                         ALU.mult))
                            nc.vector.tensor_tensor(dst, dst, sub_gain[:, :].unsqueeze(1).to_broadcast([P, 4, 128]),
                                                    ALU.mult).then_inc(heads.sem, 1)
                        elif l == 1:
                            dve.wait_ge(valued.sem, valued.nth(1, 8 * c + 7))
                            r_ = row_inv[:, b, 8 * c:8 * c + 8]
                            link(nc.vector.reciprocal(r_, row_sum[:, b, 8 * c:8 * c + 8]))
                            nc.vector.tensor_tensor(hn[:, b, 512 * c:512 * c + 512].rearrange("p (h d) -> p h d", h=8),
                                                    bank[b][:, :].rearrange("p (h d) -> p h d", h=8),
                                                    r_.unsqueeze(2).to_broadcast([P, 8, 64]),
                                                    ALU.mult).then_inc(heads.sem, 1)
                    if l == 2:
                        for b in range(TB):
                            dve.wait_ge(valued.sem, valued.nth(2, 15))
                            link(nc.vector.reciprocal(row_inv[:, b, 0:8], row_sum[:, b, 0:8]))
                            nc.vector.tensor_tensor(hn[:, b, 0:512].rearrange("p (h d) -> p h d", h=8),
                                                    bank[b][:, :].rearrange("p (h d) -> p h d", h=8),
                                                    row_inv[:, b, 0:8].unsqueeze(2).to_broadcast([P, 8, 64]),
                                                    ALU.mult).then_inc(head_o.sem, 1)
                        for b in range(TB):
                            dve.wait_ge(head_sq.sem, head_sq.nth(2, 0, b))
                            nc.vector.tensor_reduce(hst_m[:, b, 0:8], hn[:, b, 512:1024].rearrange("p (h d) -> p h d", h=8),
                                                    AX_X, ALU.add).then_inc(head_ss.sem, 1)
                            root_of(b, 8, 64, (2, 0, b), 1.0)
                            dst = hn[:, b, 0:512].rearrange("p (h d) -> p h d", h=8)
                            link(nc.vector.tensor_tensor(dst, dst, hst[:, b, 0:8].unsqueeze(2).to_broadcast([P, 8, 64]),
                                                         ALU.mult))
                            if b == 0:
                                dve.wait_ge(s_late, 16)
                            nc.vector.tensor_tensor(hn[:, b, 0:512], hn[:, b, 0:512], head_g, ALU.mult).then_inc(heads.sem, 1)

                for i in range(17):
                    if i < 16:
                        shift(i)
                    if i >= 1 and l == 0:
                        mix(i - 1)
                    if l < 2 and i == 10:
                        head_out(0)
                        turn_lo(f"att{l}", 0, 0)
                        turn_lo(f"att{l}", 1, 0)
                c = 1 if l < 2 else 0
                head_out(c)
                turn_lo(f"att{l}", 0, c)
                turn_lo(f"att{l}", 1, c)

            def feed_forward(l):
                n_it, kt, dn = ffn_shape[l]
                for j in range(n_it):
                    u = first["up", l, j]
                    split_to(u + 2 + 3)
                    for b in range(TB):
                        dve.wait_ge(act_e.sem, act_e.nth(l, j, b))
                        if l < 2:
                            link(nc.vector.tensor_scalar(e_s[:, b, 0:256], e_s[:, b, 0:256], 1.0, None, ALU.add))
                            link(nc.vector.reciprocal(e_s[:, b, 0:256], e_s[:, b, 0:256]))
                            link(nc.vector.tensor_tensor(e_s[:, b, 256:512], bank[4 + b][:, 0:256], e_s[:, b, 0:256],
                                                         ALU.mult))
                            nc.vector.tensor_tensor(a_s[:, b, 0:256], bank[4 + b][:, 256:512], e_s[:, b, 256:512],
                                                    ALU.mult).then_inc(act_a.sem, 1)
                        else:
                            nc.vector.tensor_tensor(a_s[:, b, :], bank[4 + b][:, :], e_s[:, b, :],
                                                    ALU.mult).then_inc(act_a.sem, 1)
                    split_to(u + 2 + (dn if j else 0) + 3)
                    for b in range(TB):
                        dve.wait_ge(a_hi.sem, a_hi.nth(l, j, b))
                        v = (slice(None), slice(None), slice(b * P, (b + 1) * P))
                        nc.vector.tensor_tensor(al[:, 0:256 * kt].rearrange("p (k s) -> p k s", s=S)[v],
                                                bank[6 + b][:, 0:kt * P].rearrange("p (k s) -> p k s", s=P),
                                                ah[:, 0:256 * kt].bitcast(F32).rearrange("p (k s) -> p k s", s=S)[v],
                                                ALU.subtract).then_inc(a_lo.sem, 1)
                u = first["down", l, n_it - 1] + dn
                split_to(u + 3)
                for b in range(TB):
                    if b == 0:
                        dve.wait_ge(summed.sem, summed.nth(f"dn{l}", 0))
                    else:
                        used(dve, u - 1)
                    for n in range(2):
                        nc.vector.tensor_tensor(h[:, b, 512 * n:512 * n + 512], h[:, b, 512 * n:512 * n + 512],
                                                bank[2 * b + n][:, :], ALU.add).then_inc(added.sem, 1)

            dve.wait_ge(sumsq.sem, sumsq.nth("meta", 0))
            mean_eps(mean[0:META, 30:31], stat[0:META, 30:31], D, EPS_2)
            refine(stat[0:META, 31:32], mean[0:META, 30:31], tmps[0:META, 30:31])
            nc.vector.scalar_tensor_tensor(out=meta_n, in0=meta_s, scalar=stat[0:META, 31:32], in1=meta_gain,
                                           op0=ALU.mult, op1=ALU.mult).then_inc(normed.sem, 1)
            for b in range(TB):
                norm("mix0", b)
            dve.wait_ge(turned_hi.sem, turned_hi.nth("meta", 0, 0))
            nc.vector.tensor_tensor(xl[:, :, 0:META], bank[6][:, 0:P].rearrange("p (k s) -> p k s", k=KD),
                                    xh[:, :, 0:META].bitcast(F32), ALU.subtract).then_inc(turned_lo.sem, 1)
            split_to(2)
            norm_turns("mix0")
            dve.wait_ge(s_lamv, 64)
            for m in range(2):
                ins = nc.vector.tensor_tensor_reduce(out=lam_out, in0=lams[:, 2 * m, :], in1=lams[:, 2 * m + 1, :],
                                                     scale=1.0, scalar=0.0, op0=ALU.mult, op1=ALU.add,
                                                     accum_out=lam[:, m:m + 1])
                if m == 0:
                    link(ins)
            ins.then_inc(s_lamr, 1)
            dve.wait_ge(s_dist, 1)
            link(nc.vector.tensor_copy(dist_f, dist_i))
            link(nc.vector.tensor_scalar(dist_n, dist_f, -1.0, None, ALU.mult))
            link(nc.vector.tensor_tensor(dist_f, dist_f, dist_n, ALU.max))
            for hd in range(8):
                ins = nc.vector.tensor_scalar(near[:, hd, :], dist_f, -(2.0 ** -(hd + 1)), None, ALU.mult)
            link(ins)
            dve.wait_ge(s_lamr, 2)
            nc.vector.tensor_scalar(lam[:, 0:1], lam[:, 2:3], lam[:, 3:4], LAM_INIT, ALU.subtract, ALU.add).then_inc(s_lamr, 1)
            dve.wait_ge(s_lamr, 3)

            for l in range(LAYERS):
                if l == 1:
                    norm_turns("mix1")
                for c in range(2):
                    u = first["qkv", l, c, 1]
                    split_to(u + 2 + 3)
                    used(dve, u + 1)
                    for m in range(4):
                        src = bank[2 * ((3 * c + 1) % 2) + m // 2][:, 256 * (m % 2):256 * (m % 2) + 256]
                        if l == 0:
                            ins = nc.vector.tensor_copy(k_t[:, 4 * c + m, :], src)
                        else:
                            ins = nc.vector.tensor_scalar(k_t[:, 4 * c + m, :], src, bias_q[:, 8 + 4 * c + m:9 + 4 * c + m],
                                                          None, ALU.add)
                    ins.then_inc(k_ready.sem, 1)
                    split_to(u + 4 + 3)
                    used(dve, u + 3)
                    for b in range(TB):
                        src = bank[2 * ((3 * c + 2) % 2) + b][:, :]
                        if l == 0:
                            ins = nc.vector.tensor_copy(v_s[:, b, 512 * c:512 * c + 512], src)
                        else:
                            dve.wait_ge(s_bv, 16)
                            ins = nc.vector.tensor_tensor(v_s[:, b, 512 * c:512 * c + 512], src,
                                                          bias_v[:, 512 * c:512 * c + 512], ALU.add)
                    ins.then_inc(v_ready.sem, 1)
                dve.wait_ge(emb_hi.sem, emb_hi.nth(l))
                nc.vector.tensor_tensor(al[:, 0:512], bank[6][:, :], ah[:, 0:512].bitcast(F32),
                                        ALU.subtract).then_inc(emb_lo.sem, 1)
                split_to(first["wo", l] + 4)
                if l == 1:
                    dve.wait_ge(s_near, 4)
                attention(l)
                split_to(first["wo", l] + 4 + 3)
                add_halves(f"wo{l}", first["wo", l])
                for b in range(TB):
                    norm(f"ffn{l}", b)
                split_to(first["pp", l] + 1 + 3)
                norm_turns(f"ffn{l}")
                feed_forward(l)
                for b in range(TB):
                    norm(f"ple{l}", b)
                split_to(first["gate", l] + 4)
                norm_turns(f"ple{l}")
                for n in range(2):
                    split_to(first["gate", l] + 2 * n + 2 + 3)
                    for b in range(TB):
                        dve.wait_ge(gate_e.sem, gate_e.nth(l, n, b))
                        link(nc.vector.tensor_scalar(prob[:, b, :], prob[:, b, :], 1.0, None, ALU.add))
                        link(nc.vector.reciprocal(prob[:, b, :], prob[:, b, :]))
                        link(nc.vector.tensor_tensor(prob[:, b, :], prob[:, b, :], pp[:, b, 512 * n:512 * n + 512],
                                                     ALU.mult))
                        nc.vector.tensor_tensor(h[:, b, 512 * n:512 * n + 512], h[:, b, 512 * n:512 * n + 512],
                                                prob[:, b, :], ALU.add).then_inc(added.sem, 1)
                if l == 0:
                    dve.wait_ge(s_small, 16 * 8)
                    link(nc.vector.tensor_scalar(bias_q8[:, :], bias_q[:, 0:8], HEAD_SCALE, None, ALU.mult))
                    for b in range(TB):
                        norm("mix1", b)
                else:
                    for b in range(TB):
                        norm("fin1", b, dst=h[:, b, :])
                split_to(first["gate", l] + 4 + 4)
            link(nc.vector.memset(ah[:, :].bitcast(F32), 0.0))
            link(nc.vector.memset(al[:, :].bitcast(F32), 0.0))
            link(nc.vector.tensor_copy(wf_h[:, :, 0:8], wf_raw[:, :, :]))
            nc.vector.tensor_tensor(wf_l[:, :, 0:8], wf_raw[:, :, :], wf_h[:, :, 0:8].bitcast(F32),
                                    ALU.subtract).then_inc(s_wf, 2)
            for b in range(TB):
                norm("mix2", b, eps=EPS_2)
            norm_turns("mix2")
            split_to(first["in", "k"] + 2 + 3)
            used(dve, first["in", "k"] + 1)
            for m in range(4):
                ins = nc.vector.tensor_copy(k2[:, m, :], bank[4 + m][:, 0:T])
            ins.then_inc(k_ready.sem, 1)
            split_to(first["in", "v"] + 2 + 3)
            used(dve, first["in", "v"] + 1)
            for b in range(TB):
                nc.vector.tensor_copy(v2[:, b, :], bank[b][:, :])
            nc.vector.tensor_copy(v_meta, bank[2][0:META, :])
            nc.vector.tensor_scalar(f_z, bank[3][0:8, 0:T], bf[:, 0:1], None, ALU.add).then_inc(v_ready.sem, 1)
            dve.wait_ge(v_ready.sem, v_ready.nth(2, 0))
            link(nc.vector.tensor_scalar(f_e, f_z, -1.0, None, ALU.mult))
            nc.vector.tensor_tensor(f_e, f_e, f_z, ALU.max).then_inc(s_fabs, 1)
            dve.wait_ge(s_fe, 1)
            nc.vector.tensor_scalar(f_e, f_e, 1.0, None, ALU.add).then_inc(s_f1, 1)
            dve.wait_ge(s_fl, 1)
            link(nc.vector.scalar_tensor_tensor(out=f_z, in0=f_z, scalar=0.0, in1=f_e, op0=ALU.min, op1=ALU.subtract))
            dve.wait_ge(s_consts2, 2)
            nc.vector.tensor_tensor_scan(f_c, f_one, f_z, 0.0, ALU.mult, ALU.add).then_inc(s_cum, 1)
            split_to(first["in", "u"] + 2 + 3)
            used(dve, first["in", "u"] + 1)
            dve.wait_ge(s_bc, 2)
            for m in range(4):
                ins = nc.vector.tensor_tensor(cu[:, m, :], c_s[:, m, :], bank[4 + m][:, 0:T], ALU.mult)
            ins.then_inc(s_cu, 1)
            dve.wait_ge(s_cu, 1)
            for w in range(3):
                for m in range(4):
                    src = cu[:, m, META - 2 + w:META - 2 + w + S]
                    if w == 0:
                        ins = nc.vector.tensor_scalar(y_s[:, m, :], src, conv_w[:, 0, m:m + 1], None, ALU.mult)
                    else:
                        ins = nc.vector.scalar_tensor_tensor(out=y_s[:, m, :], in0=src, scalar=conv_w[:, w, m:m + 1],
                                                             in1=y_s[:, m, :], op0=ALU.mult, op1=ALU.add)
                link(ins)
            link(nc.vector.tensor_tensor(y_s, y_s, b_s, ALU.mult))
            nc.vector.tensor_tensor(sq2, y_s, y_s, ALU.mult).then_inc(s_ysq, 1)
            split_to(first["wo", 2] + 2)
            attention(2)
            dve.wait_ge(s_ysum, 1)
            dve.wait_ge(s_yst, 1)
            for m in range(2):
                ins = nc.vector.tensor_scalar(y_m[:, 512 * m:512 * m + 512], bank[2 + m][:, :], 1.0 / 64, EPS_2,
                                              ALU.mult, ALU.add)
            link(ins)
            refine(q_reg[:, 1024:2048], y_m, y_t)
            for m in range(4):
                ins = nc.vector.scalar_tensor_tensor(out=y_s[:, m, :], in0=y_s[:, m, :], scalar=conv_g[:, m:m + 1],
                                                     in1=sq2[:, m, :], op0=ALU.mult, op1=ALU.mult)
            ins.then_inc(s_y, 1)
            dve.wait_ge(s_yh, 1)
            nc.vector.tensor_tensor(xl[:, 4:8, META:T], y_s, xh[:, 4:8, META:T].bitcast(F32),
                                    ALU.subtract).then_inc(s_yl, 1)
            split_to(first["wo", 2] + 4 + 3)
            add_halves("wo2", first["wo", 2])
            for b in range(TB):
                norm("ffn2", b, eps=EPS_2)
            norm_turns("ffn2")
            feed_forward(2)
            for b in range(TB):
                norm("fin2", b, eps=EPS_2)


LAM_INIT = 0.8 - 0.6 * math.exp(-0.3 * 0)


def kernel(**inputs):
    import numpy as _np
    import concourse.bacc as _bacc
    from concourse import mybir as _mybir
    from concourse.bass_utils import run_bass_kernel_spmd as _run

    nc = _bacc.Bacc("TRN2", target_bir_lowering=False, num_devices=1)
    arrays, dram = {}, {}
    for name, value in inputs.items():
        a = _np.ascontiguousarray(value)
        arrays[f"in_{name}_dram"] = a
        dram[name] = nc.dram_tensor(f"in_{name}_dram", a.shape, _mybir.dt.from_np(a.dtype), kind="ExternalInput").ap()
    out = nc.dram_tensor("out_0_dram", (1, S, D), _mybir.dt.float32, kind="ExternalOutput").ap()
    two_blocks_kernel(nc, dram, out)
    r = _run(nc, [arrays], core_ids=[0])
    return r.results[0]["out_0_dram"]
```

```python
import math
from contextlib import ExitStack

import concourse.bass as bass
from concourse import mybir

ALU = mybir.AluOpType
ACT = mybir.ActivationFunctionType
F32 = mybir.dt.float32
F32R = mybir.dt.float32r
I32 = mybir.dt.int32
AX_X = mybir.AxisListType.X

P = 128
D = 1024
S = 256
TB = S // P
META = 16
T = META + S
KD = D // P
UNIT = 2048
RAW = 4
RING = 4
LAYERS = 2
FFN = 2816
FF2 = 4096
EPS = 1e-6
EPS_HEAD = 1e-5
EPS_2 = 1e-5
HEAD_SCALE = 0.125
MASKED = -1e30
GRID = 64
KR, KC = 8, 16
NEAR = 384


class Order:

    def __init__(self, sem, keys):
        self.sem = sem
        self.place = {k: n + 1 for n, k in enumerate(keys)}
        assert len(self.place) == len(keys)

    def nth(self, *key):
        return self.place[key]


def two_blocks_kernel(nc, t, out):
    ctx = ExitStack()
    with ctx:
        def sb(name, shape, dt=F32):
            return ctx.enter_context(nc.sbuf_tensor(name, shape, dt))

        def sem(name):
            return ctx.enter_context(nc.semaphore(name))

        units = []

        def add_cols(w, n0, halves=(0, 1)):
            wv = w.rearrange("(k p) n -> p k n", p=P)
            for kh in halves:
                units.append([(0, 512, wv[:, 4 * kh:4 * kh + 4, n0:n0 + 512])])

        def add_gate_up(wg, wu, n0):
            g, u = (w.rearrange("(k p) n -> p k n", p=P) for w in (wg, wu))
            for kh in range(2):
                units.append([(0, 256, g[:, 4 * kh:4 * kh + 4, n0:n0 + 256]),
                              (256, 512, u[:, 4 * kh:4 * kh + 4, n0:n0 + 256])])

        def add_rows(w, k0):
            units.append([(0, 1024, w.rearrange("(k p) n -> p k n", p=P)[:, k0:k0 + 2, :])])

        first = {}
        ffn_shape = {}
        for l in range(LAYERS):
            wqkv = t["da_w_qkv"][0] if l == 0 else t["na_w_qkv"][0]
            wo = t["da_w_o"][0] if l == 0 else t["na_w_o"][0]
            for c in range(2):
                for part in range(3):
                    first["qkv", l, c, part] = len(units)
                    add_cols(wqkv, part * D + c * 512)
            first["wo", l] = len(units)
            for kh in range(2):
                for n in range(2):
                    add_cols(wo, n * 512, (kh,))
            n_it = FFN // 256
            ffn_shape[l] = (n_it, 2, 1)
            for j in range(n_it + 1):
                if j < n_it:
                    first["up", l, j] = len(units)
                    add_gate_up(t["ffn_w_gate"][l], t["ffn_w_up"][l], j * 256)
                if j >= 1:
                    first["down", l, j - 1] = len(units)
                    add_rows(t["ffn_w_down"][l], 2 * (j - 1))
            first["pp", l] = len(units)
            add_rows(t["ple_w_proj"][l], 0)
            first["gate", l] = len(units)
            for n in range(2):
                add_cols(t["ple_w_gate"][l], n * 512)
        w_in = t["w_in_2"][0]
        col_of = {"q": 0, "k": 512, "v": 1024, "f": 1536, "b": 1544, "c": 2056, "u": 2568}
        for part in "qkvbcu":
            first["in", part] = len(units)
            add_cols(w_in, col_of[part])
        first["wo", 2] = len(units)
        for kh in (1, 0):
            for n in range(2):
                add_cols(t["w_out_2"][0], n * 512, (kh,))
        n_it = FF2 // 512
        ffn_shape[2] = (n_it, 4, 2)
        for j in range(n_it + 1):
            if j < n_it:
                first["up", 2, j] = len(units)
                add_cols(t["w_ff1_2"][0], j * 512)
            if j >= 1:
                first["down", 2, j - 1] = len(units)
                add_rows(t["w_ff2_2"][0], 4 * (j - 1))
                add_rows(t["w_ff2_2"][0], 4 * (j - 1) + 2)
        NU = len(units)

        raw = sb("raw", [P, RAW, UNIT])
        wh = sb("wh", [P, RING, UNIT], F32R)
        wl = sb("wl", [P, RING, UNIT], F32R)
        h = sb("h", [P, TB, D])
        hn = sb("hn", [P, TB, D])
        xh = sb("xh", [P, KD, T], F32R)
        xl = sb("xl", [P, KD, T], F32R)
        gains = sb("gains", [P, 2, D])
        q_reg = sb("q_reg", [P, 2048])
        k_reg = sb("k_reg", [P, 2176])
        v_reg = sb("v_reg", [P, 2048])
        b_reg = sb("b_reg", [P, 16 * NEAR])
        ah = sb("ah", [P, 1024], F32R)
        al = sb("al", [P, 1024], F32R)
        p_in = sb("p_in", [P, 512])
        prob = sb("prob", [P, 3, 512])
        pt = sb("pt", [P, 2, 512])
        ident = sb("ident", [P, P])
        ones = sb("ones", [P, P])
        stat = sb("stat", [P, 48])
        rstd = sb("rstd", [P, 24])
        root_x = sb("root_x", [P, 2])
        root_m = sb("root_m", [P, 16])
        root_t = sb("root_t", [P, 16])
        r_half = sb("r_half", [P, 6, 2])
        r_sq = sb("r_sq", [P, 6, 2])
        r_cols = sb("r_cols", [P, T])
        r_two = sb("r_two", [P, 2])
        hst_m = sb("hst_m", [P, 16])
        hst = sb("hst", [P, 16])
        row_sum = sb("row_sum", [P, 2, 16])
        row_inv = sb("row_inv", [P, 2, 16])
        row_neg = sb("row_neg", [P, 3, 2])
        lam = sb("lam", [P, 4])
        bias_q = sb("bias_q", [P, 16])
        bias_q8 = sb("bias_q8", [P, 8])
        wf_raw = sb("wf_raw", [P, KD, 8])
        conv_w = sb("conv_w", [P, 3, 4])
        bf = sb("bf", [8, 1])

        bank = [ctx.enter_context(nc.psum_tensor(f"bank{i}", [P, 512], F32)) for i in range(8)]

        q_t = q_reg[:, :].rearrange("p (g s) -> p g s", g=8)
        k_t = k_reg[:, 0:2048].rearrange("p (g s) -> p g s", g=8)
        pp = k_reg[:, 0:2048].rearrange("p (b n) -> p b n", b=TB)
        v_s = v_reg[:, :].rearrange("p (b n) -> p b n", b=TB)
        near = b_reg[:, :].rearrange("p (h m) -> p h m", h=16)
        e_s = q_reg[:, 0:1024].rearrange("p (b n) -> p b n", b=TB)
        a_s = v_reg[:, 0:1024].rearrange("p (b n) -> p b n", b=TB)
        p_s = p_in[:, :].rearrange("p (b n) -> p b n", b=TB)
        lams = pt[:, 0, 0:256].rearrange("p (v d) -> p v d", v=4)
        lam_out = pt[:, 0, 256:320]
        sub_gain = sb("sub_gain", [P, 128])
        dist_i = b_reg[:, 8 * NEAR:9 * NEAR].bitcast(I32)
        dist_f = b_reg[:, 9 * NEAR:10 * NEAR]
        dist_n = b_reg[:, 10 * NEAR:11 * NEAR]
        meta_gain = v_reg[0:META, 0:D]
        grid_mask = sb("grid_mask", [P, GRID])
        bias_v = hn[:, 0, :]
        q2 = q_reg[:, 0:1024].rearrange("p (g s) -> p g s", g=4)
        conv_g = q_reg[:, 1024:1536]
        k2 = k_reg[:, 0:4 * T].rearrange("p (g s) -> p g s", g=4)
        minus = k_reg[0:8, 4 * T:4 * T + 1024].rearrange("p (h m) -> p h m", h=8)
        v2 = v_reg[:, 0:1024].rearrange("p (b n) -> p b n", b=TB)
        o = 0
        causal = b_reg[:, o:o + 2 * T].rearrange("p (b s) -> p b s", b=2); o += 2 * T
        c_s = b_reg[:, o:o + 4 * T].rearrange("p (g s) -> p g s", g=4); o += 4 * T
        b_s = b_reg[:, o:o + 1024].rearrange("p (g s) -> p g s", g=4); o += 1024
        cu = b_reg[:, o:o + 4 * T].rearrange("p (g s) -> p g s", g=4); o += 4 * T
        v_meta = b_reg[0:META, o:o + 512]; o += 512
        y_s = b_reg[:, o:o + 1024].rearrange("p (g s) -> p g s", g=4); o += 1024
        f_z = b_reg[0:8, o:o + T]; o += T
        f_e = b_reg[0:8, o:o + T]; o += T
        f_c = b_reg[0:8, o:o + T]; o += T
        assert o <= 16 * NEAR
        y_sq, head_s = (b_reg[:, k:k + 1024].rearrange("p (b n) -> p b n", b=TB)
                        for k in (2 * T, 6 * T + 1024))
        w1 = v_reg[:, :].rearrange("p (b n) -> p b n", b=TB)
        diag = pt[:, 1, 0:S]
        f_one = v_reg[0:8, 1024:1024 + T]
        head_g = p_in[:, :]
        wf_h = ah[:, :].rearrange("p (k m) -> p k m", k=KD)
        wf_l = al[:, :].rearrange("p (k m) -> p k m", k=KD)
        meta_s = k_reg[0:META, 0:D]
        meta_n = k_reg[0:META, D:2 * D]

        def tok(b):
            return slice(META + b * P, META + (b + 1) * P)

        NORMS = ["mix0", "ffn0", "ple0", "mix1", "ffn1", "ple1", "fin1", "mix2", "ffn2", "fin2"]
        BC = [(b, c) for b in range(2) for c in range(2)]
        CB = [(b, c) for c in range(2) for b in range(2)]
        TURNS = []
        for l in range(3):
            TURNS += [(f"mix{l}", *k) for k in CB] + ([("meta", 0, 0)] if l == 0 else [])
            TURNS += [(f"att{l}", b, c) for c in ((0, 1) if l < 2 else (1, 0)) for b in range(2)]
            TURNS += [(f"ffn{l}", *k) for k in CB]
            if l < 2:
                TURNS += [(f"ple{l}", *k) for k in CB]
        SQ, NRM = [], []
        for n in NORMS:
            if n == "fin1":
                SQ += [(m, b, c) for c in range(2) for m in ("fin1", "mix2") for b in range(2)]
                NRM += [(m, b, c) for c in range(2) for b in range(2) for m in ("fin1", "mix2")]
            elif n != "mix2":
                SQ += [(n, *k) for k in (BC if n == "mix0" else CB)]
                NRM += [(n, *k) for k in (CB if n in LATER else BC)]
            if n == "mix0":
                SQ.append(("meta", 0, 0))
                NRM.append(("meta", 0, 0))
        ATT = [(l, i) for l in range(3) for i in range(16)]
        ITS = [(l, j, b) for l in range(3) for j in range(ffn_shape[l][0]) for b in range(2)]

        s_raw = [sem(f"raw_landed{i}") for i in range(RAW)]
        s_hi = sem("unit_hi")
        s_lo = sem("unit_lo")
        s_used = sem("unit_used")
        sumsq = Order(sem("sumsq"), SQ)
        normed = Order(sem("normed"), NRM)
        rooted = Order(sem("rooted"), [(n,) for n in LATER if n != "mix1"])
        turned = Order(sem("turned"), TURNS)
        turned_hi = Order(sem("turned_hi"), TURNS)
        turned_lo = Order(sem("turned_lo"), TURNS)
        LC = [(l, c) for l in range(2) for c in range(2)] + [(2, 0)]
        q_ready = Order(sem("q_ready"), LC[:4])
        q_scaled = Order(sem("q_scaled"), LC[2:])
        diag_ready = Order(sem("diag_ready"), [("mix1",), ("mix2",)])
        r_spread = Order(sem("r_spread"), [("mix1",), ("mix2",)])
        r_ready = Order(sem("r_ready"), [("mix1",), ("mix2",)])
        k_ready = Order(sem("k_ready"), LC)
        v_ready = Order(sem("v_ready"), LC)
        scored = Order(sem("scored"), ATT)
        shifted = Order(sem("shifted"), ATT)
        exped = Order(sem("exped"), ATT)
        mixed = Order(sem("mixed"), [(0, i) for i in range(16)])
        p_turned = Order(sem("p_turned"), ATT)
        p_copied = Order(sem("p_copied"), ATT)
        valued = Order(sem("valued"), ATT)
        o_out0 = Order(sem("o_out0"), [(0, g) for g in range(4)])
        o_out = Order(sem("o_out"), [(1, g) for g in range(4)] + [(2, g) for g in range(2)])
        head_sq = Order(sem("head_sq"), [(0, 0), (0, 1), (0, 2), (0, 3), (2, 1), (2, 0)])
        heads = Order(sem("heads"), [(0, c, b) for c in range(2) for b in range(2)] + [(2, 1), (2, 0)])
        emb_turned = Order(sem("emb_turned"), [(l,) for l in range(2)])
        emb_hi = Order(sem("emb_hi"), [(l,) for l in range(2)])
        emb_lo = Order(sem("emb_lo"), [(l,) for l in range(2)])
        pp_done = Order(sem("pp_done"), [(l,) for l in range(2)])
        pp_ready = Order(sem("pp_ready"), [(l, b) for l in range(2) for b in range(2)])
        SUMS = []
        for l in range(3):
            SUMS += [(f"wo{l}", 0), (f"wo{l}", 1), (f"dn{l}", 0, 0), (f"dn{l}", 0, 1), (f"dn{l}", 1, 0)]
            SUMS += [(f"gt{l}", 0), (f"gt{l}", 1)] if l < 2 else []
        summed = Order(sem("summed"), SUMS)
        gate_e = Order(sem("gate_e"), [(l, n, b) for l in range(2) for n in range(2) for b in range(2)])
        RES = []
        for l in range(3):
            for stage in ("wo", "dn", "gt")[:3 if l < 2 else 2]:
                RES += [(f"{stage}{l}", n, b) for n in range(2) for b in range(2)]
        added = Order(sem("added"), RES)
        up_done = Order(sem("up_done"), [(l, j) for l in range(3) for j in range(ffn_shape[l][0])])
        act_e = Order(sem("act_e"), ITS)
        act_a = Order(sem("act_a"), ITS)
        a_turned = Order(sem("a_turned"), ITS)
        a_hi = Order(sem("a_hi"), ITS)
        a_lo = Order(sem("a_lo"), ITS)
        s_dve = sem("dve_own")
        s_act = sem("act_own")
        s_pool = sem("pool_own")
        s_pe = sem("pe_own")
        s_x = [sem(f"x_landed{b}") for b in range(TB)]
        s_gain = [sem(f"gain_landed{i}") for i in range(2)]
        s_gain_first = sem("gain_first_landed")
        s_meta = sem("meta_landed")
        s_small = sem("small_landed")
        s_lamv = sem("lambda_landed")
        s_emb = sem("emb_landed")
        s_bv = sem("bias_v_landed")
        s_rpb = sem("rpb_landed")
        s_late = sem("late_landed")
        s_ident = sem("ident_ready")
        s_dist = sem("dist_ready")
        s_near = sem("near_ready")
        s_lamr = sem("lambda_ready")
        s_consts2 = sem("consts2_ready")
        s_wf = sem("wf_ready")
        s_fdone = sem("f_product_done")
        s_fabs = sem("f_abs_ready")
        s_fe = sem("f_exp_ready")
        s_f1 = sem("f_plus_ready")
        s_fl = sem("f_log_ready")
        s_cum = sem("cum_ready")
        s_b = sem("b_copied")
        s_c = sem("c_copied")
        s_cu = sem("cu_ready")
        s_bscaled = sem("b_scaled")
        s_cscaled = sem("c_scaled")
        s_y = sem("y_ready")
        s_yturned = sem("y_turned")
        s_residual = sem("residual_normed")
        s_store = sem("stored")

        def used(eng, u):
            eng.wait_ge(s_used, u + 1)

        def wait(eng, order, *key):
            eng.wait_ge(order.sem, order.nth(*key))

        def turn_bank(name, b, c):
            if (name, c) == ("att2", 1):
                return bank[2 + b]
            if name in ("att0", "att1") and c == 0:
                return bank[b]
            return bank[6 + b]

        SLOTS = 12
        GROUP = (4, 4, 8)

        block = ctx.enter_context(nc.Block())

        @block.sync
        def _(sp):
            for b in range(TB):
                sp.dma_start(h[:, b, :], t["x"][0].rearrange("(b p) n -> p b n", p=P)[:, b, :]).then_inc(s_x[b], 16)
            for i in range(NU):
                if i >= RAW:
                    sp.wait_ge(s_lo, i - RAW + 1)
                dst = raw[:, i % RAW, :]
                dst = dst.rearrange("p (k n) -> p k n", n=1024 if units[i][0][1] == 1024 else 512)
                for c0, c1, src in units[i]:
                    sp.dma_start(dst[:, :, c0:c1], src).then_inc(s_raw[i % RAW], 16)
            for b in range(TB):
                wait(sp, normed, "fin2", b, 1)
                sp.dma_start(out[0].rearrange("(b p) n -> p b n", p=P)[:, b, :], hn[:, b, :]).then_inc(s_store, 16)
            sp.wait_ge(s_store, 16 * TB)

        landed = []
        count = [0] * RAW
        for i in range(NU):
            count[i % RAW] += 16 * len(units[i])
            landed.append(count[i % RAW])

        @block.gpsimd
        def _(pool):
            own = [0]

            def link(ins):
                own[0] += 1
                ins.then_inc(s_pool, 1)
                pool.wait_ge(s_pool, own[0])

            gain_of = [t["norm_mix"][0], t["norm_ffn"][0], t["norm_ple"][0], t["norm_mix"][1], t["norm_ffn"][1],
                       t["norm_ple"][1], t["norm_final"], t["norm_mix_g_2"][0], t["norm_mlp_g_2"][0],
                       t["final_norm_g_2"]]

            def load_gain(n):
                if n >= 2:
                    wait(pool, normed, NORMS[n - 2], 1, 1)
                pool.dma_start(gains[:, n % 2, :], gain_of[n].partition_broadcast(P)).then_inc(s_gain[n % 2], 16)

            link(nc.gpsimd.memset(ident[:, :], 0.0))
            nc.gpsimd.affine_select(out=ident[:, :], in_=ident[:, :], compare_op=ALU.not_equal, fill=1.0, base=0,
                                    pattern=[[-1, P]], channel_multiplier=1).then_inc(s_ident, 1)
            nc.gpsimd.iota(dist_i, pattern=[[-1, NEAR]], base=P, channel_multiplier=1).then_inc(s_dist, 1)
            load_gain(1)
            for v, name in enumerate(("da_lambda_q1", "da_lambda_k1", "da_lambda_q2", "da_lambda_k2")):
                pool.dma_start(lams[:, v, :], t[name][0].partition_broadcast(P)).then_inc(s_lamv, 16)
            pool.dma_start(sub_gain[:, :], t["da_subln"][0].partition_broadcast(P)).then_inc(s_small, 16)
            pool.dma_start(p_s, t["p"][0, 0].rearrange("(b p) n -> p b n", p=P)).then_inc(s_emb, 16)
            with nc.allow_non_contiguous_dma("biases and convolution weights, a few KB"):
                pool.dma_start(bias_q[:, :], t["na_b_qkv"][0, 0:2 * D].rearrange("(g p) -> p g", p=P)).then_inc(s_small, 16)
                pool.dma_start(wf_raw[:, :, :], w_in.rearrange("(k p) n -> p k n", p=P)[:, :, col_of["f"]:col_of["f"] + 8]).then_inc(s_small, 16)
                for w in range(3):
                    pool.dma_start(conv_w[:, w, :], t["conv_w_2"][0, w].rearrange("(g p) -> p g", p=P)).then_inc(s_small, 16)
                pool.dma_start(bf[:, :], t["b_f_2"].rearrange("a h -> h a")).then_inc(s_small, 16)
            link(nc.gpsimd.memset(grid_mask[:, :], 0.0))
            for r in range(2):
                half = grid_mask[GRID * r:GRID * r + GRID, :]
                low, high = half[:, 0:GRID - KC], half[:, KC:GRID]
                link(nc.gpsimd.affine_select(out=low, in_=low, compare_op=ALU.is_ge, fill=MASKED, base=KC // 2,
                                             pattern=[[1, GRID - KC]], channel_multiplier=-1))
                link(nc.gpsimd.affine_select(out=high, in_=high, compare_op=ALU.is_ge, fill=MASKED,
                                             base=KC // 2 - 1 - KC, pattern=[[-1, GRID - KC]], channel_multiplier=1))
            nc.gpsimd.memset(r_cols[:, 0:META], 1.0).then_inc(s_ident, 1)
            pool.wait_ge(s_ident, 2)
            nc.gpsimd.memset(ones[:, :], 1.0).then_inc(s_ident, 1)

            load_gain(2)
            wait(pool, shifted, 0, 15)
            rpb = t["na_rpb"]
            for r in range(2):
                for c in range(GRID):
                    src = bass.AP(tensor=rpb.tensor, offset=(5 - r) * 31 + KC - 1 - c,
                                  ap=[[15 * 31, 16], [31, 6], [1, GRID]])
                    row = GRID * r + c
                    pool.dma_start(near[row:row + 1, :, :].rearrange("p h (j c) -> p h j c", c=GRID),
                                   src.unsqueeze(0)).then_inc(s_rpb, 16)
            wait(pool, head_sq, 0, 3)
            pool.dma_start(p_s, t["p"][1, 0].rearrange("(b p) n -> p b n", p=P)).then_inc(s_emb, 16)
            load_gain(3)
            pool.wait_ge(s_rpb, 16 * P)
            for hd in range(0, 16, 4):
                part = b_reg[:, hd * NEAR:(hd + 4) * NEAR].rearrange("p (j c) -> p j c", c=GRID)
                nc.gpsimd.tensor_tensor(part, part, grid_mask[:, :].unsqueeze(1).to_broadcast([P, 24, GRID]),
                                        ALU.add).then_inc(s_near, 1)
            pool.wait_ge(s_near, 4)
            load_gain(4)
            wait(pool, turned, "mix1", 1, 1)
            pool.dma_start(bias_v, t["na_b_qkv"][0, 2 * D:3 * D].partition_broadcast(P)).then_inc(s_bv, 16)
            load_gain(5)
            load_gain(6)
            load_gain(7)
            wait(pool, added, "gt1", 1, 1)
            wait(pool, q_scaled, 2, 0)
            pool.dma_start(conv_g, t["out_norm_g_2"][0, 512:1024].partition_broadcast(P)).then_inc(s_late, 16)
            pool.dma_start(head_g, t["out_norm_g_2"][0, 0:512].partition_broadcast(P)).then_inc(s_late, 16)
            link(nc.gpsimd.memset(b_reg[:, 0:2 * T], 0.0))
            for b in range(2):
                link(nc.gpsimd.affine_select(out=causal[:, b, :], in_=causal[:, b, :], compare_op=ALU.is_ge,
                                             fill=MASKED, base=P * b + META, pattern=[[-1, T]],
                                             channel_multiplier=1))
            link(nc.gpsimd.memset(minus, 0.0))
            nc.gpsimd.affine_select(out=minus, in_=minus, compare_op=ALU.not_equal, fill=-1.0, base=0,
                                    pattern=[[-1, 8], [0, P]], channel_multiplier=1).then_inc(s_consts2, 1)
            pool.wait_ge(s_consts2, 1)
            pool.wait_ge(s_residual, 1)
            nc.gpsimd.memset(f_one, 1.0).then_inc(s_consts2, 1)
            load_gain(8)
            pool.wait_ge(s_b, 1)
            nc.gpsimd.tensor_tensor(b_s, b_s, r_cols[:, META:T].unsqueeze(1).to_broadcast([P, 4, S]),
                                    ALU.mult).then_inc(s_bscaled, 1)
            pool.wait_ge(s_c, 1)
            for step in range(2):
                nc.gpsimd.tensor_tensor(c_s, c_s, r_cols[:, :].unsqueeze(1).to_broadcast([P, 4, T]),
                                        ALU.mult).then_inc(s_cscaled, 1)
                pool.wait_ge(s_cscaled, step + 1)
            load_gain(9)

        @block.scalar
        def _(act):
            own = [0]
            split = [0]

            def link(ins):
                own[0] += 1
                ins.then_inc(s_act, 1)
                act.wait_ge(s_act, own[0])

            def split_to(n):
                while split[0] < min(n, NU):
                    i = split[0]
                    act.wait_ge(s_raw[i % RAW], landed[i])
                    if i >= RING:
                        used(act, i - RING)
                    nc.scalar.activation(wh[:, i % RING, :], raw[:, i % RAW, :], ACT.Copy).then_inc(s_hi, 1)
                    split[0] += 1

            def square(name, b, c, junk, src=h):
                i = 4 * NORMS.index(name) + 2 * b + c
                nc.scalar.activation(junk, src[:, b, 512 * c:512 * c + 512], ACT.Square, scale=D ** -0.5,
                                     accum_out=stat[:, i:i + 1]).then_inc(sumsq.sem, 1)

            def squares_and_turns(stage, name, c):
                for b in range(TB):
                    i = 2 * c + b
                    wait(act, added, stage, c, b)
                    square(name, b, c, prob[:, i, :] if i < 3 else pt[:, 0, :])
                    turn_hi(name, b, c)

            def turn_hi(name, b, c):
                wait(act, turned, name, b, c)
                nc.scalar.activation(xh[:, 4 * c:4 * c + 4, tok(b)],
                                     turn_bank(name, b, c)[:, :].rearrange("p (k s) -> p k s", k=4),
                                     ACT.Copy).then_inc(turned_hi.sem, 1)

            def turns_hi(name, c):
                for b in range(TB):
                    turn_hi(name, b, c)

            act.dma_start(gains[:, 0, :], t["norm_mix"][0].partition_broadcast(P)).then_inc(s_gain_first, 16)
            act.dma_start(meta_s, t["meta_tokens_2"]).then_inc(s_meta, 16)
            act.dma_start(meta_gain, t["norm_mix_g_2"][0].partition_broadcast(META)).then_inc(s_meta, 16)
            for b in range(TB):
                act.wait_ge(s_x[b], 16)
                for c in range(2):
                    square("mix0", b, c, hn[:, b, 512 * c:512 * c + 512])
            split_to(1)
            turns_hi("mix0", 0)
            split_to(2)
            turns_hi("mix0", 1)
            split_to(3)
            act.wait_ge(s_meta, 32)
            nc.scalar.activation(meta_n, meta_s, ACT.Square, scale=D ** -0.5,
                                 accum_out=stat[0:META, 40:41]).then_inc(sumsq.sem, 1)
            split_to(4)
            wait(act, turned, "meta", 0, 0)
            nc.scalar.activation(xh[:, :, 0:META], bank[6][:, 0:P].rearrange("p (k s) -> p k s", k=KD),
                                 ACT.Copy).then_inc(turned_hi.sem, 1)
            act.wait_ge(s_lamr, 1)
            nc.scalar.activation(lam[:, 2:4], lam[:, 0:2], ACT.Exp).then_inc(s_lamr, 1)

            def attention_step(l, s):
                if s < 16:
                    g, b = s // 2, s % 2
                    wait(act, shifted, l, s)
                    if l < 2:
                        for m in range(2):
                            ins = nc.scalar.activation(prob[:, s % 3, 256 * m:256 * m + 256], prob[:, s % 3, 256 * m:256 * m + 256],
                                                       ACT.Exp, scale=-1.0, bias=row_neg[:, s % 3, m:m + 1],
                                                       accum_out=row_sum[:, b, 2 * g + m:2 * g + m + 1])
                        ins.then_inc(exped.sem, 1)
                    else:
                        n = META + P * (b + 1)
                        nc.scalar.activation(prob[:, s % 3, 0:n], prob[:, s % 3, 0:n], ACT.Exp, scale=-1.0,
                                             bias=row_neg[:, s % 3, 0:1],
                                             accum_out=row_sum[:, b, g:g + 1]).then_inc(exped.sem, 1)
                i = s - 2
                if 0 <= i < 16:
                    wait(act, p_turned, l, i)
                    if i >= 2:
                        wait(act, valued, l, i - 2)
                    src = bank[6]
                    if l == 0:
                        ins = nc.scalar.activation(pt[:, i % 2, 0:256], src[:, 0:256], ACT.Copy)
                    elif l == 1:
                        ins = nc.scalar.activation(pt[:, i % 2, :], src[:, :], ACT.Copy)
                    else:
                        n = P * (i % 2 + 1)
                        nc.scalar.activation(pt[0:META, i % 2, 256:384], src[0:META, 256:384], ACT.Copy)
                        ins = nc.scalar.activation(pt[:, i % 2, 0:n], src[:, 0:n], ACT.Copy)
                    ins.then_inc(p_copied.sem, 1)
                e = s - 3
                if l == 0 and 0 <= e < 16 and e % 4 == 3:
                    g = e // 4
                    wait(act, valued, 0, e)
                    nc.scalar.activation(hn[:, :, 256 * g:256 * g + 256],
                                         bank[7][:, :].rearrange("p (b n) -> p b n", b=TB), ACT.Copy).then_inc(o_out0.sem, 1)
                    wait(act, o_out0, 0, g)
                    if g == 0:
                        wait(act, emb_turned, 0)
                    else:
                        wait(act, head_sq, 0, g - 1)
                    for b in range(TB):
                        for m in range(2):
                            at, col = P * (2 * b + m), 4 * b + 2 * (g % 2) + m
                            ins = nc.scalar.activation(p_in[:, at:at + P], hn[:, b, P * (2 * g + m):P * (2 * g + m + 1)],
                                                       ACT.Square, accum_out=hst_m[:, 8 * (g // 2) + col:8 * (g // 2) + col + 1])
                    ins.then_inc(head_sq.sem, 1)

            def spread_root(name, src):
                wait(act, r_spread, name)
                nc.scalar.activation(r_cols[:, META:T], src[:, 0:S], ACT.Copy).then_inc(r_ready.sem, 1)

            def feed_forward(l):
                n_it, kt, dn = ffn_shape[l]
                name = f"ffn{l}"
                for j in range(n_it):
                    u = first["up", l, j]
                    if j == 0:
                        squares_and_turns(f"wo{l}", name, 0)
                        squares_and_turns(f"wo{l}", name, 1)
                    split_to(u + 2 + 3)
                    for b in range(TB):
                        if j == 0:
                            wait(act, rooted, name)
                        if b == 0:
                            wait(act, up_done, l, j)
                        else:
                            used(act, u + 1)
                        if l < 2:
                            ins = nc.scalar.activation(e_s[:, b, 0:256], bank[4 + b][:, 0:256], ACT.Tanh,
                                                       scale=r_half[:, LATER.index(name), b:b + 1])
                        else:
                            ins = nc.scalar.activation(e_s[:, b, :], bank[4 + b][:, :], ACT.Relu)
                        ins.then_inc(act_e.sem, 1)
                    split_to(u + 2 + (dn if j else 0) + 3)
                    for b in range(TB):
                        wait(act, a_turned, l, j, b)
                        nc.scalar.activation(ah[:, 0:256 * kt].rearrange("p (k s) -> p k s", s=S)[:, :, b * P:(b + 1) * P],
                                             bank[6 + b][:, 0:kt * P].rearrange("p (k s) -> p k s", s=P),
                                             ACT.Copy).then_inc(a_hi.sem, 1)
                split_to(first["down", l, n_it - 1] + dn + 3)

            for l in range(LAYERS):

                def q_out(c):
                    if l == 0:
                        used(act, first["qkv", l, c, 0] + 1)
                    else:
                        wait(act, q_scaled, l, c)
                    for m in range(4):
                        src = bank[2 * (c % 2) + m // 2][:, 256 * (m % 2):256 * (m % 2) + 256]
                        if l == 0:
                            ins = nc.scalar.activation(q_t[:, 4 * c + m, :], src, ACT.Copy, scale=HEAD_SCALE)
                        else:
                            q = q_t[:, 4 * c + m, :]
                            ins = nc.scalar.activation(q, q, ACT.Identity, scale=HEAD_SCALE,
                                                       bias=bias_q8[:, 4 * c + m:4 * c + m + 1])
                    ins.then_inc(q_ready.sem, 1)

                u = first["qkv", l, 0, 0]
                split_to(u + 2 + 3)
                if l == 1:
                    spread_root("mix1", bank[4])
                q_out(0)
                split_to(u + 6 + 3)
                wait(act, emb_turned, l)
                nc.scalar.activation(ah[:, 512:1024], bank[6][:, :], ACT.Copy).then_inc(emb_hi.sem, 1)
                for slot in range(SLOTS):
                    if slot % 2 == 0:
                        split_to(u + 6 + slot // 2 + 4)
                    if slot == 3:
                        q_out(1)
                    if slot >= 1:
                        attention_step(l, slot - 1)
                for s in range(SLOTS - 1, 19):
                    attention_step(l, s)
                    if s == 16:
                        split_to(first["wo", l] + 4)
                    if s == (13 if l == 0 else 12):
                        turns_hi(f"att{l}", 0)
                if l == 1:
                    split_to(first["wo", l] + 1 + 4)
                turns_hi(f"att{l}", 1)
                split_to(first["wo", l] + 2 + 4)
                feed_forward(l)
                name = f"ple{l}"

                def pp_out(b):
                    if b == 0:
                        wait(act, pp_done, l)
                    else:
                        used(act, first["pp", l])
                    for n in range(2):
                        ins = nc.scalar.activation(pp[:, b, 512 * n:512 * n + 512], bank[4 + n][:, :], ACT.Copy, scale=0.5)
                    ins.then_inc(pp_ready.sem, 1)

                pp_out(0)
                wait(act, sumsq, f"ffn{l}", 1, 1)
                squares_and_turns(f"dn{l}", name, 0)
                pp_out(1)
                squares_and_turns(f"dn{l}", name, 1)
                split_to(first["gate", l] + 4)
                for n in range(2):
                    u = first["gate", l] + 2 * n
                    if n == 1:
                        turns_hi(f"mix{l + 1}", 0)
                    split_to(u + (5 if n == 0 else 4))
                    for b in range(TB):
                        if n == 0:
                            wait(act, rooted, name)
                        if b == 0:
                            wait(act, summed, f"gt{l}", n)
                        else:
                            used(act, u + 1)
                            wait(act, sumsq, name, 1, 1)
                        if n == 1:
                            wait(act, added, f"gt{l}", 0, b)
                        nc.scalar.activation(prob[:, b, :], bank[2 * b if n == 0 else 4 + b][:, :], ACT.Tanh,
                                             scale=r_half[:, LATER.index(name), b:b + 1]).then_inc(gate_e.sem, 1)
                    for b in range(TB):
                        wait(act, added, f"gt{l}", n, b)
                        at = 512 * (2 * n + b)
                        square("mix1" if l == 0 else "fin1", b, n, q_reg[:, at:at + 512])
                    if l == 1:
                        for b in range(TB):
                            wait(act, normed, "fin1", b, n)
                            at = 2 * T + 512 * (2 * n + b)
                            square("mix2", b, n, b_reg[:, at:at + 512], w1)
                turns_hi(f"mix{l + 1}", 1)
                split_to(first["gate", l] + 4 + 4)
            u = first["in", "q"]
            split_to(u + 5)
            spread_root("mix2", bank[2])
            split_to(first["in", "v"] + 4)
            act.wait_ge(s_fabs, 1)
            nc.scalar.activation(f_e, f_e, ACT.Exp, scale=-1.0).then_inc(s_fe, 1)
            act.wait_ge(s_f1, 1)
            nc.scalar.activation(f_e, f_e, ACT.Ln).then_inc(s_fl, 1)
            split_to(first["in", "v"] + 2 + 3)
            u = first["in", "b"]
            for slot in range(SLOTS):
                if slot % 2 == 0:
                    split_to(u + slot // 2 + 4)
                if slot == 3:
                    used(act, u + 1)
                    for m in range(4):
                        ins = nc.scalar.activation(b_s[:, m, :], bank[6 + m // 2][:, 256 * (m % 2):256 * (m % 2) + 256], ACT.Copy)
                    ins.then_inc(s_b, 1)
                if slot == 7:
                    used(act, u + 3)
                    for m in range(4):
                        ins = nc.scalar.activation(c_s[:, m, :], bank[m][:, 0:T], ACT.Copy)
                    ins.then_inc(s_c, 1)
                if slot >= 2:
                    attention_step(2, slot - 2)
            for s in range(SLOTS - 2, 19):
                attention_step(2, s)
                if s == 14:
                    split_to(first["wo", 2] + 4)
                if s == 14:
                    act.wait_ge(s_yturned, 1)
                    for b in range(TB):
                        nc.scalar.activation(hn[:, b, 512:1024], bank[b][:, :], ACT.Copy)
                        ins = nc.scalar.activation(y_sq[:, b, :], bank[b][:, :], ACT.Square)
                    ins.then_inc(head_sq.sem, 1)
                if s == 17:
                    turns_hi("att2", 1)
            wait(act, o_out, 2, 1)
            for b in range(TB):
                ins = nc.scalar.activation(head_s[:, b, :], hn[:, b, 0:512], ACT.Square)
            ins.then_inc(head_sq.sem, 1)
            turns_hi("att2", 0)
            split_to(first["wo", 2] + 2 + 4)
            feed_forward(2)
            for c in range(2):
                for b in range(TB):
                    wait(act, added, "dn2", c, b)
                    square("fin2", b, c, hn[:, b, 512 * c:512 * c + 512])

        @block.tensor
        def _(pe):
            def unit(u):
                pe.wait_ge(s_lo, u + 1)
                return wh[:, u % RING, :], wl[:, u % RING, :]

            def three(dst, lhs, rhs, start, stop):
                (lh, ll), (rh, rl) = lhs, rhs
                nc.tensor.matmul(dst, lh, rh, start=start, stop=False, skip_group_check=True)
                nc.tensor.matmul(dst, lh, rl, start=False, stop=False, skip_group_check=True)
                return nc.tensor.matmul(dst, ll, rh, start=False, stop=stop, skip_group_check=True)

            def x_of(k, cols):
                return xh[:, k, cols], xl[:, k, cols]

            def need(name, b, c):
                wait(pe, turned_lo, name, b, c)

            def turn(name, b, c):
                if c == 1 and not name.startswith("att"):
                    need(name, b, 0)
                for k in range(4):
                    ins = nc.tensor.transpose(turn_bank(name, b, c)[:, k * P:(k + 1) * P],
                                              hn[:, b, (4 * c + k) * P:(4 * c + k + 1) * P], ident[:, :])
                ins.then_inc(turned.sem, 1)

            def norm_turns(name, c):
                for b in range(TB):
                    wait(pe, normed, name, b, c)
                    turn(name, b, c)

            def tokens_unit(u, kh, banks, name, first_kh, last_kh, cols=(tok(0), tok(1)), signal=None):
                w_hi, w_lo = (w.rearrange("p (k n) -> p k n", k=4) for w in unit(u))
                for b, c in enumerate(cols):
                    if name and b < TB:
                        need(name, b, kh)
                    for k in range(4):
                        ins = three(banks[b][:, :], x_of(4 * kh + k, c), (w_hi[:, k, :], w_lo[:, k, :]),
                                    kh == first_kh and k == 0, kh == last_kh and k == 3)
                    if b == len(cols) - 1:
                        ins.then_inc(s_used, 1)
                    elif b == 0 and kh == last_kh and signal:
                        ins.then_inc(signal, 1)
                    yield

            def features_unit(u, kh, dst, shared, cols, name):
                w_hi, w_lo = (w.rearrange("p (k n) -> p k n", k=4) for w in unit(u))
                for b in range(TB):
                    need(name, b, kh)
                for m in range(4):
                    cleared = shared and m % 2 == 1
                    for k in range(4):
                        ins = three(dst(m), (w_hi[:, k, m * P:(m + 1) * P], w_lo[:, k, m * P:(m + 1) * P]),
                                    x_of(4 * kh + k, cols), kh == 0 and k == 0 and not cleared,
                                    kh == 1 and k == 3)
                    if m == 3:
                        ins.then_inc(s_used, 1)
                    if m % 2 == 1:
                        yield

            def run(steps):
                for _ in steps:
                    pass

            def spread_root(name, dst):
                wait(pe, diag_ready, name)
                pe.wait_ge(s_ident, 3)
                nc.tensor.matmul(dst[:, 0:S], ones[:, :], diag, start=True, stop=True).then_inc(r_spread.sem, 1)

            def pair(first_bank):
                return lambda m: bank[first_bank + m // 2][:, 256 * (m % 2):256 * (m % 2) + 256]

            def attention_step(l, s):
                if s < 16:
                    g, b = s // 2, s % 2
                    if l < 2:
                        if s >= 1:
                            wait(pe, shifted, l, s - 1)
                        if s in (0, 8):
                            wait(pe, q_ready, l, s // 8)
                            wait(pe, k_ready, l, s // 8)
                        for m in range(2):
                            half = slice(64 * m, 64 * m + 64)
                            ins = nc.tensor.matmul(bank[4 + m][:, 0:256], q_t[half, g, b * P:(b + 1) * P],
                                                   k_t[half, g, :], start=True, stop=True)
                    else:
                        if s >= 2:
                            wait(pe, shifted, 2, s - 2)
                        n = META + P * (b + 1)
                        half = slice(64 * (g % 2), 64 * (g % 2) + 64)
                        dst = bank[4 + s % 2]
                        nc.tensor.matmul(dst[:, 0:n], minus[:, g, :], f_c[:, 0:n], start=True, stop=False).then_inc(s_pe, 1)
                        pe.wait_ge(s_pe, s + 1)
                        ins = nc.tensor.matmul(dst[:, 0:n], q2[half, g // 2, b * P:(b + 1) * P], k2[half, g // 2, 0:n],
                                               start=False, stop=True)
                    ins.then_inc(scored.sem, 1)
                i = s - 2
                if 0 <= i < 16:
                    b = i % 2
                    if l == 0:
                        wait(pe, mixed, 0, i)
                    else:
                        wait(pe, exped, l, i)
                    if i >= 1:
                        wait(pe, p_copied, l, i - 1)
                    dst = bank[6]
                    if l < 2:
                        for m in range(1 if l == 0 else 2):
                            for kb in range(2):
                                cols = slice(256 * m + P * kb, 256 * m + P * kb + P)
                                ins = nc.tensor.transpose(dst[:, cols], prob[:, i % 3, cols], ident[:, :])
                    else:
                        nc.tensor.transpose(dst[0:META, 256:384], prob[:, i % 3, 0:META], ident[:, :])
                        for kb in range(b + 1):
                            ins = nc.tensor.transpose(dst[:, P * kb:P * kb + P],
                                                      prob[:, i % 3, META + P * kb:META + P * kb + P], ident[:, :])
                    ins.then_inc(p_turned.sem, 1)
                i = s - 3
                if 0 <= i < 16:
                    g, b = i // 2, i % 2
                    wait(pe, p_copied, l, i)
                    if i in (0, 8) and l < 2:
                        wait(pe, v_ready, l, i // 8)
                    if i % GROUP[l] == 0 and i:
                        wait(pe, o_out0 if l == 0 else o_out, l, i // GROUP[l] - 1)
                    if l == 0:
                        dst = bank[7][:, 256 * b + P * (g % 2):256 * b + P * (g % 2) + P]
                        for kb in range(2):
                            ins = nc.tensor.matmul(dst, pt[:, b, P * kb:P * kb + P], v_s[:, kb, P * g:P * g + P],
                                                   start=(kb == 0), stop=(kb == 1))
                    elif l == 1:
                        for m in range(2):
                            hd = 2 * g + m
                            dst = bank[7][:, 256 * b + 64 * (hd % 4):256 * b + 64 * (hd % 4) + 64]
                            for kb in range(2):
                                ins = nc.tensor.matmul(dst, pt[:, b, 256 * m + P * kb:256 * m + P * kb + P],
                                                       v_s[:, kb, 64 * hd:64 * hd + 64],
                                                       start=(kb == 0), stop=(kb == 1))
                    else:
                        dst = bank[7][:, 256 * b + 64 * (g % 4):256 * b + 64 * (g % 4) + 64]
                        for kb in range(b + 1):
                            nc.tensor.matmul(dst, pt[:, b, P * kb:P * kb + P], v2[:, kb, 64 * g:64 * g + 64],
                                             start=(kb == 0), stop=False)
                        ins = nc.tensor.matmul(dst, pt[0:META, b, 256:384], v_meta[:, 64 * g:64 * g + 64],
                                               start=False, stop=True)
                    ins.then_inc(valued.sem, 1)

            def feed_forward(l):
                n_it, kt, dn = ffn_shape[l]
                name = f"ffn{l}"
                for j in range(n_it + 1):
                    if j < n_it:
                        if j >= 1:
                            for b in range(TB):
                                wait(pe, act_a, l, j - 1, b)
                        u = first["up", l, j]
                        run(tokens_unit(u, 0, (bank[4], bank[5]), name, 0, 1, signal=up_done.sem))
                        if j == 0:
                            norm_turns(name, 1)
                        run(tokens_unit(u + 1, 1, (bank[4], bank[5]), name, 0, 1, signal=up_done.sem))
                    if j >= 1:
                        for d in range(dn):
                            w_hi, w_lo = (w.rearrange("p (k n) -> p k n", k=2) for w in unit(first["down", l, j - 1] + d))
                            last = j == n_it and d == dn - 1
                            parts = [(b, k, n) for b in range(TB) for k in range(2) for n in range(2)]
                            if last:
                                parts = [(b, k, n) for n in range(2) for b in range(TB) for k in range(2)]
                            for at, (b, k, n) in enumerate(parts):
                                if d == 0:
                                    wait(pe, a_lo, l, j - 1, b)
                                cols = slice(S * (2 * d + k) + b * P, S * (2 * d + k) + (b + 1) * P)
                                ins = three(bank[2 * b + n][:, :], (ah[:, cols], al[:, cols]),
                                            (w_hi[:, k, 512 * n:512 * n + 512], w_lo[:, k, 512 * n:512 * n + 512]),
                                            j == 1 and d == 0 and k == 0, last and k == 1)
                                if at == 7:
                                    ins.then_inc(s_used, 1)
                                elif last and k == 1:
                                    ins.then_inc(summed.sem, 1)
                    if j < n_it:
                        for b in range(TB):
                            wait(pe, act_a, l, j, b)
                            if j >= 1:
                                wait(pe, a_lo, l, j - 1, b)
                            for k in range(kt):
                                ins = nc.tensor.transpose(bank[6 + b][:, k * P:(k + 1) * P],
                                                          a_s[:, b, k * P:(k + 1) * P], ident[:, :])
                            ins.then_inc(a_turned.sem, 1)

            def meta_turn():
                wait(pe, normed, "meta", 0, 0)
                for k in range(KD):
                    ins = nc.tensor.transpose(bank[6][:, META * k:META * k + META], meta_n[:, k * P:(k + 1) * P],
                                              ident[0:META, 0:META])
                ins.then_inc(turned.sem, 1)

            pe.wait_ge(s_ident, 1)
            for l in range(LAYERS):
                mix = f"mix{l}"
                if l == 0:
                    norm_turns(mix, 0)
                x_cols = slice(META, T)

                def qkv_units(c):
                    for part in range(3):
                        i = 3 * c + part
                        if i >= 2:
                            wait(pe, (q_ready, k_ready, v_ready)[(i - 2) % 3], l, (i - 2) // 3)
                        u = first["qkv", l, c, part]
                        b0 = 2 * (i % 2)
                        for kh in range(2):
                            if i == 0 and kh == 1:
                                norm_turns(mix, 1)
                            if part < 2:
                                yield from features_unit(u + kh, kh, pair(b0), True, x_cols, mix)
                            else:
                                yield from tokens_unit(u + kh, kh, (bank[b0], bank[b0 + 1]), mix, 0, 1)
                        if l == 0 and i == 0:
                            meta_turn()
                        if l == 1 and i == 0:
                            spread_root(mix, bank[4])

                run(qkv_units(0))
                pe.wait_ge(s_emb, 16 * (l + 1))
                if l == 0:
                    need("meta", 0, 0)
                for b in range(TB):
                    for k in range(2):
                        ins = nc.tensor.transpose(bank[6][:, S * k + b * P:S * k + (b + 1) * P],
                                                  p_s[:, b, k * P:(k + 1) * P], ident[:, :])
                ins.then_inc(emb_turned.sem, 1)
                for slot, _ in enumerate(qkv_units(1)):
                    if slot == 2:
                        wait(pe, emb_lo, l)
                    if slot >= 1:
                        attention_step(l, slot - 1)

                def wo_units(kh):
                    for n in range(2):
                        yield from tokens_unit(first["wo", l] + 2 * kh + n, kh, (bank[n], bank[2 + n]), f"att{l}", 0, 1,
                                               signal=summed.sem)

                def head_turns(c):
                    for b in range(TB):
                        if l == 0:
                            wait(pe, heads, 0, c, b)
                        else:
                            wait(pe, o_out, 1, 2 * c + 1)
                        turn(f"att{l}", b, c)

                wo_first = wo_units(0)
                for s in range(SLOTS - 1, 19):
                    attention_step(l, s)
                    if s == (13 if l == 0 else 12):
                        head_turns(0)
                    if s in (15, 17):
                        next(wo_first)
                run(wo_first)
                head_turns(1)
                run(tokens_unit(first["wo", l] + 2, 1, (bank[0], bank[2]), f"att{l}", 0, 1, signal=summed.sem))
                last = tokens_unit(first["wo", l] + 3, 1, (bank[1], bank[3]), f"att{l}", 0, 1, signal=summed.sem)
                next(last)
                norm_turns(f"ffn{l}", 0)
                run(last)
                feed_forward(l)
                name = f"ple{l}"
                w_hi, w_lo = (w.rearrange("p (k n) -> p k n", k=2) for w in unit(first["pp", l]))
                for b in range(TB):
                    if b == 1:
                        norm_turns(name, 0)
                        wait(pe, pp_ready, l, 0)
                    for n in range(2):
                        for k in range(2):
                            cols = slice(512 + S * k + b * P, 512 + S * k + (b + 1) * P)
                            ins = three(bank[4 + n][:, :], (ah[:, cols], al[:, cols]),
                                        (w_hi[:, k, 512 * n:512 * n + 512], w_lo[:, k, 512 * n:512 * n + 512]),
                                        k == 0, k == 1)
                    ins.then_inc(pp_done.sem if b == 0 else s_used, 1)
                norm_turns(name, 1)
                for n in range(2):
                    for kh in range(2):
                        steps = tokens_unit(first["gate", l] + 2 * n + kh, kh,
                                            (bank[0], bank[2]) if n == 0 else (bank[4], bank[5]),
                                            name, 0, 1, signal=summed.sem)
                        if n == 1 and kh == 1:
                            next(steps)
                            norm_turns(f"mix{l + 1}", 0)
                        run(steps)
            every, x_cols = slice(0, T), slice(META, T)
            run(features_unit(first["in", "q"], 0, pair(0), True, x_cols, "mix2"))
            norm_turns("mix2", 1)
            run(features_unit(first["in", "q"] + 1, 1, pair(0), True, x_cols, "mix2"))
            for kh in range(2):
                run(features_unit(first["in", "k"] + kh, kh, lambda m: bank[4 + m][:, 0:T], False, every, "mix2"))
                if kh == 0:
                    spread_root("mix2", bank[2])
            pe.wait_ge(s_wf, 2)
            for k in range(KD):
                ins = three(bank[3][:, 0:T], (wf_h[:, k, :], wf_l[:, k, :]), x_of(k, every), k == 0, k == KD - 1)
            ins.then_inc(s_fdone, 1)
            wait(pe, q_scaled, 2, 0)
            for kh in range(2):
                run(tokens_unit(first["in", "v"] + kh, kh, (bank[0], bank[1], bank[2]), "mix2", 0, 1,
                                (tok(0), tok(1), slice(0, P))))
            wait(pe, k_ready, 2, 0)
            pe.wait_ge(s_consts2, 2)

            def bcu_units():
                for i, part in enumerate("bcu"):
                    if i == 1:
                        pe.wait_ge(s_b, 1)
                        wait(pe, v_ready, 2, 0)
                    if i == 2:
                        pe.wait_ge(s_c, 1)
                    for kh in range(2):
                        if i == 0:
                            yield from features_unit(first["in", part] + kh, kh, pair(6), True, x_cols, "mix2")
                        else:
                            yield from features_unit(first["in", part] + kh, kh, lambda m: bank[m][:, 0:T], False,
                                                     every, "mix2")

            for slot, _ in enumerate(bcu_units()):
                if slot == 2:
                    pe.wait_ge(s_cum, 1)
                if slot >= 2:
                    attention_step(2, slot - 2)
            for s in range(SLOTS - 2, 19):
                attention_step(2, s)
                if s == 14:
                    pe.wait_ge(s_y, 1)
                    for b in range(TB):
                        for m in range(4):
                            ins = nc.tensor.transpose(bank[b][:, m * P:(m + 1) * P], y_s[:, m, b * P:(b + 1) * P],
                                                      ident[:, :])
                    ins.then_inc(s_yturned, 1)
                if s == 17:
                    wait(pe, heads, 2, 1)
                    for b in range(TB):
                        turn("att2", b, 1)
            for n in range(2):
                run(tokens_unit(first["wo", 2] + n, 1, (bank[n], bank[n + 2]), "att2", 1, 0))
            wait(pe, heads, 2, 0)
            for b in range(TB):
                turn("att2", b, 0)
            for n in range(2):
                run(tokens_unit(first["wo", 2] + 2 + n, 0, (bank[n], bank[n + 2]), "att2", 1, 0, signal=summed.sem))
            norm_turns("ffn2", 0)
            feed_forward(2)

        @block.vector
        def _(dve):
            own = [0]
            split = [0]

            def link(ins):
                own[0] += 1
                ins.then_inc(s_dve, 1)
                dve.wait_ge(s_dve, own[0])

            def split_to(n):
                while split[0] < min(n, NU):
                    i = split[0]
                    dve.wait_ge(s_hi, i + 1)
                    nc.vector.tensor_tensor(wl[:, i % RING, :], raw[:, i % RAW, :],
                                            wh[:, i % RING, :].bitcast(F32), ALU.subtract).then_inc(s_lo, 1)
                    split[0] += 1

            def inv_root(y, x):
                rows, n = x.shape
                m, t_ = root_m[0:rows, 0:n], root_t[0:rows, 0:n]
                nc.vector.tensor_scalar(m, x, -0.5, None, ALU.mult)
                link(nc.vector.tensor_scalar(y.bitcast(I32), x.bitcast(I32), -0.5, float(0x5F3759DF), ALU.mult, ALU.add))
                for step in range(3):
                    if n == 1:
                        link(nc.vector.scalar_tensor_tensor(out=t_, in0=y, scalar=m, in1=y, op0=ALU.mult, op1=ALU.mult))
                    else:
                        link(nc.vector.tensor_tensor(t_, y, y, ALU.mult))
                        link(nc.vector.tensor_tensor(t_, t_, m, ALU.mult))
                    link(nc.vector.scalar_tensor_tensor(out=y, in0=t_, scalar=1.5, in1=y, op0=ALU.add, op1=ALU.mult))

            def gain_there(i):
                if i == 0:
                    dve.wait_ge(s_gain_first, 16)
                else:
                    dve.wait_ge(s_gain[i % 2], 16 * ((i + 1) // 2))

            def row_roots(name, eps):
                i = NORMS.index(name)
                wait(dve, sumsq, name, 1, 1)
                parts = stat[:, 4 * i:4 * i + 4].rearrange("p (b c) -> p b c", b=TB)
                link(nc.vector.scalar_tensor_tensor(out=root_x[:, :], in0=parts[:, :, 0], scalar=eps, in1=parts[:, :, 1],
                                                    op0=ALU.add, op1=ALU.add))
                r_ = rstd[:, 2 * i:2 * i + 2]
                inv_root(r_, root_x[:, :])
                return r_

            def first_root(b, eps):
                wait(dve, sumsq, "mix0", b, 1)
                link(nc.vector.tensor_scalar(root_x[:, b:b + 1], stat[:, 2 * b:2 * b + 1], stat[:, 2 * b + 1:2 * b + 2], eps,
                                             ALU.add, ALU.add))
                inv_root(rstd[:, b:b + 1], root_x[:, b:b + 1])
                return rstd[:, b:b + 1]

            def norm(name, b, r_):
                i = NORMS.index(name)
                if b == 0:
                    gain_there(i)
                for c in range(2):
                    cols = slice(512 * c, 512 * c + 512)
                    nc.vector.scalar_tensor_tensor(out=hn[:, b, cols], in0=h[:, b, cols],
                                                   scalar=r_, in1=gains[:, i % 2, cols], op0=ALU.mult,
                                                   op1=ALU.mult).then_inc(normed.sem, 1)

            def scale_half(name, b, c, src=h, dst=hn):
                i = NORMS.index(name)
                if b == 0 and c == 0:
                    gain_there(i)
                cols = slice(512 * c, 512 * c + 512)
                nc.vector.tensor_tensor(dst[:, b, cols], src[:, b, cols], gains[:, i % 2, cols],
                                        ALU.mult).then_inc(normed.sem, 1)

            def late_roots(name, eps, factor):
                i = LATER.index(name)
                r_ = row_roots(name, eps)
                nc.vector.tensor_scalar(r_half[:, i, :], r_, 0.5, None, ALU.mult)
                nc.vector.scalar_tensor_tensor(out=r_sq[:, i, :], in0=r_, scalar=factor, in1=r_, op0=ALU.mult,
                                               op1=ALU.mult).then_inc(rooted.sem, 1)

            def diagonal(name, r_):
                for b in range(TB):
                    ins = nc.vector.tensor_scalar(diag[:, b * P:(b + 1) * P], ident[:, :], r_[:, b:b + 1], None, ALU.mult)
                ins.then_inc(diag_ready.sem, 1)

            def turn_lo(name, b, c):
                wait(dve, turned_hi, name, b, c)
                dst = (slice(None), slice(4 * c, 4 * c + 4), tok(b))
                nc.vector.tensor_tensor(xl[dst], turn_bank(name, b, c)[:, :].rearrange("p (k s) -> p k s", k=4),
                                        xh[dst].bitcast(F32), ALU.subtract).then_inc(turned_lo.sem, 1)

            def turns_lo(name, c):
                for b in range(TB):
                    turn_lo(name, b, c)

            def add_scale(stage, name, done):
                for n in range(2):
                    for b in range(TB):
                        done(n, b)
                        nc.vector.tensor_tensor(h[:, b, 512 * n:512 * n + 512], h[:, b, 512 * n:512 * n + 512],
                                                bank[2 * b + n][:, :], ALU.add).then_inc(added.sem, 1)
                        if name:
                            wait(dve, added, stage, n, b)
                            scale_half(name, b, n)
                        if stage in ("wo0", "wo1") and (n, b) == (1, 0):
                            turns_lo(name, 0)

            def done_half(stage, units_of):
                def done(n, b):
                    if b == 0:
                        wait(dve, summed, stage, n)
                    else:
                        used(dve, units_of[n])
                return done

            def attention_step(l, s):
                if s < 16:
                    g, b = s // 2, s % 2
                    wait(dve, scored, l, s)
                    if s >= 3:
                        wait(dve, p_turned, l, s - 3)
                    if l < 2:
                        for m in range(2):
                            hd = g if l == 0 else 2 * g + m
                            ins = nc.vector.tensor_tensor_reduce(
                                out=prob[:, s % 3, 256 * m:256 * m + 256], in0=bank[4 + m][:, 0:256],
                                in1=near[:, hd, P - P * b:P - P * b + 256], scale=-1.0, scalar=3.0e38,
                                op0=ALU.add, op1=ALU.min, accum_out=row_neg[:, s % 3, m:m + 1])
                        ins.then_inc(shifted.sem, 1)
                    else:
                        n = META + P * (b + 1)
                        nc.vector.tensor_tensor_reduce(
                            out=prob[:, s % 3, 0:n], in0=bank[4 + s % 2][:, 0:n], in1=causal[:, b, 0:n], scale=-1.0,
                            scalar=3.0e38, op0=ALU.add, op1=ALU.min,
                            accum_out=row_neg[:, s % 3, 0:1]).then_inc(shifted.sem, 1)
                i = s - 1
                if l == 0 and 0 <= i < 16:
                    g, b = i // 2, i % 2
                    wait(dve, exped, 0, i)
                    r_ = row_inv[:, b, 2 * g:2 * g + 2]
                    link(nc.vector.reciprocal(r_, row_sum[:, b, 2 * g:2 * g + 2]))
                    link(nc.vector.tensor_scalar(prob[:, i % 3, 256:512], prob[:, i % 3, 256:512],
                                                 r_[:, 1:2], lam[:, 0:1], ALU.mult, ALU.mult))
                    nc.vector.scalar_tensor_tensor(out=prob[:, i % 3, 0:256], in0=prob[:, i % 3, 0:256],
                                                   scalar=r_[:, 0:1], in1=prob[:, i % 3, 256:512],
                                                   op0=ALU.mult, op1=ALU.subtract).then_inc(mixed.sem, 1)
                e = s - 3
                if l > 0 and 0 <= e < 16 and e % GROUP[l] == GROUP[l] - 1:
                    g = e // GROUP[l]
                    wait(dve, valued, l, e)
                    r_ = row_inv[:, :, 4 * g:4 * g + 4]
                    link(nc.vector.reciprocal(r_, row_sum[:, :, 4 * g:4 * g + 4]))
                    for b in range(TB):
                        ins = nc.vector.tensor_tensor(
                            hn[:, b, 256 * g:256 * g + 256].rearrange("p (h d) -> p h d", h=4),
                            bank[7][:, 256 * b:256 * b + 256].rearrange("p (h d) -> p h d", h=4),
                            r_[:, b, :].unsqueeze(2).to_broadcast([P, 4, 64]), ALU.mult)
                    ins.then_inc(o_out.sem, 1)

            def head_roots(c):
                wait(dve, head_sq, 0, 2 * c + 1)
                g2 = (1.0 - LAM_INIT) ** 2
                m = hst_m[:, 8 * c:8 * c + 8]
                link(nc.vector.tensor_scalar(m, m, 1.0 / (P * g2), EPS_HEAD / g2, ALU.mult, ALU.add))
                inv_root(hst[:, 8 * c:8 * c + 8], m)

            def head_norms(c):
                if c == 0:
                    dve.wait_ge(s_small, 16 * 7)
                for b in range(TB):
                    for m in range(4):
                        dst = hn[:, b, 512 * c + P * m:512 * c + P * (m + 1)]
                        at = 8 * c + 4 * b + m
                        ins = nc.vector.scalar_tensor_tensor(out=dst, in0=dst, scalar=hst[:, at:at + 1],
                                                             in1=sub_gain[:, :], op0=ALU.mult, op1=ALU.mult)
                    ins.then_inc(heads.sem, 1)

            def second_head_stats(c, squares):
                wait(dve, head_sq, 2, c)
                for b in range(TB):
                    ins = nc.vector.tensor_reduce(hst_m[:, 8 * b:8 * b + 8],
                                                  squares[:, b, :].rearrange("p (h d) -> p h d", h=8), AX_X, ALU.add)
                link(ins)
                link(nc.vector.tensor_scalar(hst_m[:, :], hst_m[:, :], 1.0 / 64, EPS_2, ALU.mult, ALU.add))
                inv_root(hst[:, :], hst_m[:, :])

            def second_head_norms(c, gain):
                for b in range(TB):
                    half = hn[:, b, 512 * c:512 * c + 512]
                    dst = half.rearrange("p (h d) -> p h d", h=8)
                    link(nc.vector.tensor_tensor(dst, dst, hst[:, 8 * b:8 * b + 8].unsqueeze(2).to_broadcast([P, 8, 64]),
                                                 ALU.mult))
                    if b == 0:
                        dve.wait_ge(s_late, 32)
                    ins = nc.vector.tensor_tensor(half, half, gain, ALU.mult)
                ins.then_inc(heads.sem, 1)

            def feed_forward(l):
                n_it, kt, dn = ffn_shape[l]
                name = f"ffn{l}"
                i_ = LATER.index(name)
                for j in range(n_it):
                    u = first["up", l, j]
                    if j == 0:
                        if l == 2:
                            turns_lo(name, 0)
                        turns_lo(name, 1)
                        late_roots(name, EPS if l < 2 else EPS_2, 0.5 if l < 2 else 1.0)
                    split_to(u + 2 + (1 if j == 0 else 3))
                    for b in range(TB):
                        wait(dve, act_e, l, j, b)
                        if l < 2:
                            link(nc.vector.scalar_tensor_tensor(out=e_s[:, b, 256:512], in0=e_s[:, b, 0:256], scalar=1.0,
                                                                in1=bank[4 + b][:, 0:256], op0=ALU.add, op1=ALU.mult))
                            nc.vector.scalar_tensor_tensor(out=a_s[:, b, 0:256], in0=e_s[:, b, 256:512],
                                                           scalar=r_sq[:, i_, b:b + 1], in1=bank[4 + b][:, 256:512],
                                                           op0=ALU.mult, op1=ALU.mult).then_inc(act_a.sem, 1)
                        else:
                            nc.vector.scalar_tensor_tensor(out=a_s[:, b, :], in0=e_s[:, b, :],
                                                           scalar=r_sq[:, i_, b:b + 1], in1=bank[4 + b][:, :],
                                                           op0=ALU.mult, op1=ALU.mult).then_inc(act_a.sem, 1)
                    split_to(u + 2 + (dn if j else 0) + 3)
                    for b in range(TB):
                        wait(dve, a_hi, l, j, b)
                        v = (slice(None), slice(None), slice(b * P, (b + 1) * P))
                        nc.vector.tensor_tensor(al[:, 0:256 * kt].rearrange("p (k s) -> p k s", s=S)[v],
                                                bank[6 + b][:, 0:kt * P].rearrange("p (k s) -> p k s", s=P),
                                                ah[:, 0:256 * kt].bitcast(F32).rearrange("p (k s) -> p k s", s=S)[v],
                                                ALU.subtract).then_inc(a_lo.sem, 1)
                u = first["down", l, n_it - 1] + dn
                split_to(u + 3)

                def done(n, b):
                    if (n, b) == (1, 1):
                        used(dve, u - 1)
                    else:
                        wait(dve, summed, f"dn{l}", n, b)
                add_scale(f"dn{l}", f"ple{l}" if l < 2 else None, done)

            for b in range(TB):
                norm("mix0", b, first_root(b, EPS))
            split_to(1)
            turns_lo("mix0", 0)
            split_to(2)
            turns_lo("mix0", 1)
            split_to(3)
            wait(dve, sumsq, "meta", 0, 0)
            dve.wait_ge(s_meta, 32)
            link(nc.vector.tensor_scalar(stat[0:META, 40:41], stat[0:META, 40:41], EPS_2, None, ALU.add))
            inv_root(rstd[0:META, 20:21], stat[0:META, 40:41])
            nc.vector.scalar_tensor_tensor(out=meta_n, in0=meta_s, scalar=rstd[0:META, 20:21], in1=meta_gain,
                                           op0=ALU.mult, op1=ALU.mult).then_inc(normed.sem, 1)
            split_to(4)
            wait(dve, turned_hi, "meta", 0, 0)
            nc.vector.tensor_tensor(xl[:, :, 0:META], bank[6][:, 0:P].rearrange("p (k s) -> p k s", k=KD),
                                    xh[:, :, 0:META].bitcast(F32), ALU.subtract).then_inc(turned_lo.sem, 1)
            dve.wait_ge(s_lamv, 64)
            for m in range(2):
                ins = nc.vector.tensor_tensor_reduce(out=lam_out, in0=lams[:, 2 * m, :], in1=lams[:, 2 * m + 1, :],
                                                     scale=1.0, scalar=0.0, op0=ALU.mult, op1=ALU.add,
                                                     accum_out=lam[:, m:m + 1])
                if m == 0:
                    link(ins)
            ins.then_inc(s_lamr, 1)
            dve.wait_ge(s_dist, 1)
            link(nc.vector.tensor_copy(dist_f, dist_i))
            link(nc.vector.tensor_scalar(dist_n, dist_f, -1.0, None, ALU.mult))
            link(nc.vector.tensor_tensor(dist_f, dist_f, dist_n, ALU.max))
            for hd in range(8):
                ins = nc.vector.tensor_scalar(near[:, hd, :], dist_f, -(2.0 ** -(hd + 1)), None, ALU.mult)
            link(ins)
            dve.wait_ge(s_lamr, 2)
            nc.vector.tensor_scalar(lam[:, 0:1], lam[:, 2:3], lam[:, 3:4], LAM_INIT, ALU.subtract, ALU.add).then_inc(s_lamr, 1)
            dve.wait_ge(s_lamr, 3)

            for l in range(LAYERS):

                def over_rms(dst, c, part):
                    for m in range(0, 4, 2):
                        src = bank[2 * ((3 * c + part) % 2) + m // 2]
                        ins = nc.vector.tensor_tensor(dst[:, 4 * c + m:4 * c + m + 2, :],
                                                      src[:, :].rearrange("p (g s) -> p g s", g=2),
                                                      r_cols[:, META:T].unsqueeze(1).to_broadcast([P, 2, S]), ALU.mult)
                    return ins

                def q_over_rms(c):
                    if l == 1:
                        used(dve, first["qkv", l, c, 0] + 1)
                        wait(dve, r_ready, "mix1")
                        over_rms(q_t, c, 0).then_inc(q_scaled.sem, 1)

                def k_out(c):
                    used(dve, first["qkv", l, c, 1] + 1)
                    if l == 1:
                        link(over_rms(k_t, c, 1))
                    for m in range(4):
                        src = bank[2 * ((3 * c + 1) % 2) + m // 2][:, 256 * (m % 2):256 * (m % 2) + 256]
                        if l == 0:
                            ins = nc.vector.tensor_copy(k_t[:, 4 * c + m, :], src)
                        else:
                            src = k_t[:, 4 * c + m, :]
                            ins = nc.vector.tensor_scalar(k_t[:, 4 * c + m, :], src, bias_q[:, 8 + 4 * c + m:9 + 4 * c + m],
                                                          None, ALU.add)
                    ins.then_inc(k_ready.sem, 1)

                def v_out(c):
                    used(dve, first["qkv", l, c, 2] + 1)
                    for b in range(TB):
                        src = bank[2 * ((3 * c + 2) % 2) + b][:, :]
                        if l == 0:
                            ins = nc.vector.tensor_copy(v_s[:, b, 512 * c:512 * c + 512], src)
                        else:
                            dve.wait_ge(s_bv, 16)
                            r_ = rstd[:, 2 * NORMS.index("mix1") + b:2 * NORMS.index("mix1") + b + 1]
                            ins = nc.vector.scalar_tensor_tensor(out=v_s[:, b, 512 * c:512 * c + 512], in0=src, scalar=r_,
                                                                 in1=bias_v[:, 512 * c:512 * c + 512], op0=ALU.mult,
                                                                 op1=ALU.add)
                    ins.then_inc(v_ready.sem, 1)

                u = first["qkv", l, 0, 0]
                split_to(u + 2 + 3)
                q_over_rms(0)
                split_to(u + 4 + 3)
                k_out(0)
                split_to(u + 6 + 3)
                v_out(0)
                wait(dve, emb_hi, l)
                nc.vector.tensor_tensor(al[:, 512:1024], bank[6][:, :], ah[:, 512:1024].bitcast(F32),
                                        ALU.subtract).then_inc(emb_lo.sem, 1)
                if l == 1:
                    dve.wait_ge(s_near, 4)
                for slot in range(SLOTS):
                    if slot % 2 == 0:
                        split_to(u + 6 + slot // 2 + 4)
                    if slot == 3:
                        q_over_rms(1)
                    if slot == 7:
                        k_out(1)
                    if slot >= 1:
                        attention_step(l, slot - 1)
                v_out(1)
                for s in range(SLOTS - 1, 19):
                    attention_step(l, s)
                    if s == 16:
                        split_to(first["wo", l] + 4)
                    if s == 11 and l == 0:
                        head_roots(0)
                    if s == 12 and l == 0:
                        head_norms(0)
                    if s == (13 if l == 0 else 12):
                        turns_lo(f"att{l}", 0)
                if l == 1:
                    split_to(first["wo", l] + 1 + 4)
                if l == 0:
                    head_roots(1)
                    head_norms(1)
                turns_lo(f"att{l}", 1)
                split_to(first["wo", l] + 2 + 4)
                add_scale(f"wo{l}", f"ffn{l}", done_half(f"wo{l}", [first["wo", l] + 2, first["wo", l] + 3]))
                feed_forward(l)
                name = f"ple{l}"
                turns_lo(name, 0)
                turns_lo(name, 1)
                split_to(first["gate", l] + 4)
                late_roots(name, EPS, 1.0)
                for n in range(2):
                    if n == 1:
                        turns_lo(f"mix{l + 1}", 0)
                    split_to(first["gate", l] + (5 if n == 0 else 6))
                    for b in range(TB):
                        wait(dve, gate_e, l, n, b)
                        if n == 0:
                            wait(dve, pp_ready, l, b)
                        link(nc.vector.scalar_tensor_tensor(out=prob[:, b, :], in0=prob[:, b, :], scalar=1.0,
                                                            in1=pp[:, b, 512 * n:512 * n + 512], op0=ALU.add,
                                                            op1=ALU.mult))
                        nc.vector.tensor_tensor(h[:, b, 512 * n:512 * n + 512], h[:, b, 512 * n:512 * n + 512],
                                                prob[:, b, :], ALU.add).then_inc(added.sem, 1)
                        wait(dve, added, f"gt{l}", n, b)
                        if l == 0:
                            scale_half("mix1", b, n)
                        else:
                            scale_half("fin1", b, n, dst=w1)
                            wait(dve, normed, "fin1", b, n)
                            scale_half("mix2", b, n, src=w1)
                if l == 0:
                    link(nc.vector.tensor_scalar(bias_q8[:, :], bias_q[:, 0:8], HEAD_SCALE, None, ALU.mult))
                turns_lo(f"mix{l + 1}", 1)
                split_to(first["gate", l] + 7)
                if l == 0:
                    diagonal("mix1", row_roots("mix1", EPS))
                else:
                    r1 = row_roots("fin1", EPS)
                    parts = stat[:, 28:32].rearrange("p (b c) -> p b c", b=TB)
                    wait(dve, sumsq, "mix2", 1, 1)
                    link(nc.vector.tensor_tensor(root_x[:, :], parts[:, :, 0], parts[:, :, 1], ALU.add))
                    link(nc.vector.tensor_tensor(root_x[:, :], root_x[:, :], r1, ALU.mult))
                    link(nc.vector.tensor_tensor(root_x[:, :], root_x[:, :], r1, ALU.mult))
                    link(nc.vector.tensor_scalar(root_x[:, :], root_x[:, :], EPS_2, None, ALU.add))
                    r2 = rstd[:, 14:16]
                    inv_root(r2, root_x[:, :])
                    link(nc.vector.tensor_tensor(r_two[:, :], r1, r2, ALU.mult))
                    diagonal("mix2", r_two)
                    for b in range(TB):
                        ins = nc.vector.tensor_scalar(h[:, b, :], w1[:, b, :], r1[:, b:b + 1], None, ALU.mult)
                    ins.then_inc(s_residual, 1)
                split_to(first["gate", l] + 4 + 4)
            link(nc.vector.memset(ah[:, :].bitcast(F32), 0.0))
            link(nc.vector.memset(al[:, :].bitcast(F32), 0.0))
            link(nc.vector.tensor_copy(wf_h[:, :, 0:8], wf_raw[:, :, :]))
            nc.vector.tensor_tensor(wf_l[:, :, 0:8], wf_raw[:, :, :], wf_h[:, :, 0:8].bitcast(F32),
                                    ALU.subtract).then_inc(s_wf, 2)
            split_to(first["in", "q"] + 2 + 3)
            wait(dve, r_ready, "mix2")
            used(dve, first["in", "q"] + 1)
            for m in range(2):
                ins = nc.vector.scalar_tensor_tensor(out=q2[:, 2 * m:2 * m + 2, :],
                                                     in0=bank[m][:, :].rearrange("p (g s) -> p g s", g=2),
                                                     scalar=HEAD_SCALE,
                                                     in1=r_cols[:, META:T].unsqueeze(1).to_broadcast([P, 2, S]),
                                                     op0=ALU.mult, op1=ALU.mult)
            ins.then_inc(q_scaled.sem, 1)
            split_to(first["in", "k"] + 2 + 3)
            used(dve, first["in", "k"] + 1)
            for m in range(4):
                ins = nc.vector.tensor_tensor(k2[:, m, :], bank[4 + m][:, 0:T], r_cols[:, :], ALU.mult)
            ins.then_inc(k_ready.sem, 1)
            dve.wait_ge(s_fdone, 1)
            link(nc.vector.tensor_tensor(f_z, bank[3][0:8, 0:T], r_cols[0:8, :], ALU.mult))
            link(nc.vector.tensor_scalar(f_z, f_z, bf[:, 0:1], None, ALU.add))
            link(nc.vector.tensor_scalar(f_e, f_z, -1.0, None, ALU.mult))
            nc.vector.tensor_tensor(f_e, f_e, f_z, ALU.max).then_inc(s_fabs, 1)
            dve.wait_ge(s_fe, 1)
            nc.vector.tensor_scalar(f_e, f_e, 1.0, None, ALU.add).then_inc(s_f1, 1)
            dve.wait_ge(s_fl, 1)
            link(nc.vector.scalar_tensor_tensor(out=f_z, in0=f_z, scalar=0.0, in1=f_e, op0=ALU.min, op1=ALU.subtract))
            dve.wait_ge(s_consts2, 2)
            nc.vector.tensor_tensor_scan(f_c, f_one, f_z, 0.0, ALU.mult, ALU.add).then_inc(s_cum, 1)
            split_to(first["in", "v"] + 2 + 3)
            used(dve, first["in", "v"] + 1)
            for b in range(TB):
                nc.vector.tensor_scalar(v2[:, b, :], bank[b][:, :], r_two[:, b:b + 1], None, ALU.mult)
            nc.vector.tensor_copy(v_meta, bank[2][0:META, :]).then_inc(v_ready.sem, 1)
            u = first["in", "b"]
            for slot in range(SLOTS):
                if slot % 2 == 0:
                    split_to(u + slot // 2 + 4)
                if slot >= 2:
                    attention_step(2, slot - 2)
            for s in range(SLOTS - 2, 19):
                attention_step(2, s)
                if s == 14:
                    split_to(first["wo", 2] + 4)
                if s == 10:
                    used(dve, first["in", "u"] + 1)
                    dve.wait_ge(s_cscaled, 2)
                    for m in range(4):
                        ins = nc.vector.tensor_tensor(cu[:, m, :], c_s[:, m, :], bank[m][:, 0:T], ALU.mult)
                    ins.then_inc(s_cu, 1)
                    dve.wait_ge(s_cu, 1)
                if s in (11, 12, 13):
                    w = s - 11
                    for m in range(4):
                        src = cu[:, m, META - 2 + w:META - 2 + w + S]
                        if w == 0:
                            ins = nc.vector.tensor_scalar(y_s[:, m, :], src, conv_w[:, 0, m:m + 1], None, ALU.mult)
                        else:
                            ins = nc.vector.scalar_tensor_tensor(out=y_s[:, m, :], in0=src, scalar=conv_w[:, w, m:m + 1],
                                                                 in1=y_s[:, m, :], op0=ALU.mult, op1=ALU.add)
                    link(ins)
                if s == 13:
                    dve.wait_ge(s_bscaled, 1)
                    nc.vector.tensor_tensor(y_s, y_s, b_s, ALU.mult).then_inc(s_y, 1)
                if s == 15:
                    second_head_stats(1, y_sq)
                if s == 16:
                    second_head_norms(1, conv_g)
                if s == 17:
                    turns_lo("att2", 1)
            second_head_stats(0, head_s)
            second_head_norms(0, head_g)
            turns_lo("att2", 0)
            split_to(first["wo", 2] + 2 + 4)
            add_scale("wo2", "ffn2", done_half("wo2", [first["wo", 2] + 2, first["wo", 2] + 3]))
            feed_forward(2)
            r_ = row_roots("fin2", EPS_2)
            for b in range(TB):
                norm("fin2", b, r_[:, b:b + 1])


LAM_INIT = 0.8 - 0.6 * math.exp(-0.3 * 0)
LATER = ["ffn0", "ple0", "mix1", "ffn1", "ple1", "ffn2"]


def kernel(**inputs):
    import numpy as _np
    import concourse.bacc as _bacc
    from concourse import mybir as _mybir
    from concourse.bass_utils import run_bass_kernel_spmd as _run

    nc = _bacc.Bacc("TRN2", target_bir_lowering=False, num_devices=1, dynamic_dma_scratch_size=8192)
    arrays, dram = {}, {}
    for name, value in inputs.items():
        a = _np.ascontiguousarray(value)
        arrays[f"in_{name}_dram"] = a
        dram[name] = nc.dram_tensor(f"in_{name}_dram", a.shape, _mybir.dt.from_np(a.dtype), kind="ExternalInput").ap()
    out = nc.dram_tensor("out_0_dram", (1, S, D), _mybir.dt.float32, kind="ExternalOutput").ap()
    two_blocks_kernel(nc, dram, out)
    r = _run(nc, [arrays], core_ids=[0])
    return r.results[0]["out_0_dram"]
```
